# Optimizing a Trainium2 kernel written in Bass

```python
import math
import jax, jax.numpy as jnp
from jax import lax
import numpy as np

D_MODEL = 1024
BATCH = 1
SEQ = 256
DEPTH = 4

N_MIXERS = 3
BLOCK = 128
ROPE_THETA = 10000.0
NORM_EPS = 1e-5
D_FF = 4 * D_MODEL

A_HEAD_DIM = 64
A_N_HEADS = D_MODEL // A_HEAD_DIM
A_N_KV_HEADS = A_N_HEADS // 8
A_WINDOW = 128
A_Q_DIM = A_N_HEADS * A_HEAD_DIM
A_KV_DIM = A_N_KV_HEADS * A_HEAD_DIM

SSM_D_INNER = 2 * D_MODEL
SSM_HEAD_DIM = 64
SSM_N_HEADS = SSM_D_INNER // SSM_HEAD_DIM
SSM_N_GROUPS = 8
SSM_HEADS_PER_GROUP = SSM_N_HEADS // SSM_N_GROUPS
SSM_D_STATE = 128
SSM_CONV = 4
SSM_CHUNK = 128
SSM_BC_DIM = SSM_N_GROUPS * SSM_D_STATE
SSM_CONV_DIM = SSM_D_INNER + 2 * SSM_BC_DIM
SSM_IN_DIM = SSM_D_INNER + SSM_CONV_DIM + SSM_N_HEADS

C_HEAD_DIM = 64
C_HEADS_PER_GROUP = D_MODEL // C_HEAD_DIM
C_PATTERNS = ((128, 1), (512, 4), (2048, 16))
C_N_GROUPS = len(C_PATTERNS)
C_QKV_DIM = 3 * C_N_GROUPS * C_HEADS_PER_GROUP * C_HEAD_DIM

N_A = (DEPTH + 2) // 3
N_B = (DEPTH + 1) // 3
N_C = DEPTH // 3

kernel_name = "hybrid_swa_mamba2_dilated_trunk"

def rmsnorm(x, w):
    xf = x.astype(jnp.float32)
    y = xf * lax.rsqrt(jnp.mean(xf * xf, axis=-1, keepdims=True) + NORM_EPS)
    return (y * w.astype(jnp.float32)).astype(x.dtype)

def rope(t, positions):
    half = t.shape[-1] // 2
    inv = ROPE_THETA ** (-jnp.arange(half, dtype=jnp.float32) / half)
    ang = positions.astype(jnp.float32)[..., None] * inv
    cos = jnp.cos(ang)[:, :, None, :]
    sin = jnp.sin(ang)[:, :, None, :]
    tf = t.astype(jnp.float32)
    t1, t2 = tf[..., :half], tf[..., half:]
    return jnp.concatenate([t1 * cos - t2 * sin, t2 * cos + t1 * sin], axis=-1).astype(t.dtype)

def banded_attention(q, k, v, max_dist, sinks=None):
    n, L, H, Dh = q.shape
    Hkv = k.shape[2]
    R = H // Hkv
    nb = -(-L // BLOCK)
    pad = nb * BLOCK - L
    padw = ((0, 0), (0, pad), (0, 0), (0, 0))
    qb = jnp.pad(q, padw).reshape(n, nb, BLOCK, Hkv, R, Dh)
    kb = jnp.pad(k, padw).reshape(n, nb, BLOCK, Hkv, Dh)
    vb = jnp.pad(v, padw).reshape(n, nb, BLOCK, Hkv, Dh)

    def with_prev(t):
        prev = jnp.pad(t, ((0, 0), (1, 0), (0, 0), (0, 0), (0, 0)))[:, :-1]
        return jnp.concatenate([prev, t], axis=2)

    kk, vv = with_prev(kb), with_prev(vb)
    s = jnp.einsum('nbqgrd,nbkgd->nbgrqk', qb, kk,
                   preferred_element_type=jnp.float32) * (Dh ** -0.5)
    blk = jnp.arange(nb)[:, None, None] * BLOCK
    qpos = blk + jnp.arange(BLOCK)[None, :, None]
    kpos = blk - BLOCK + jnp.arange(2 * BLOCK)[None, None, :]
    dist = qpos - kpos
    mask = (dist >= 0) & (dist <= max_dist) & (kpos >= 0)
    s = jnp.where(mask[None, :, None, None], s, -jnp.inf)
    m = jnp.max(s, axis=-1)
    if sinks is not None:
        sk = sinks.astype(jnp.float32).reshape(Hkv, R)[None, None, :, :, None]
        m = jnp.maximum(m, sk)
    p = jnp.exp(s - m[..., None])
    denom = jnp.sum(p, axis=-1)
    if sinks is not None:
        denom = denom + jnp.exp(sk - m)
    lse = m + jnp.log(denom)
    o = jnp.einsum('nbgrqk,nbkgd->nbqgrd', (p / denom[..., None]).astype(v.dtype), vv)
    o = o.reshape(n, nb * BLOCK, H, Dh)[:, :L]
    lse = jnp.transpose(lse, (0, 1, 4, 2, 3)).reshape(n, nb * BLOCK, H)[:, :L]
    return o, lse

def swa_sink_mixer(h, positions, w_qkv, b_qkv, sinks, w_o, b_o):
    B, S, _ = h.shape
    qkv = h @ w_qkv + b_qkv
    q = qkv[..., :A_Q_DIM].reshape(B, S, A_N_HEADS, A_HEAD_DIM)
    k = qkv[..., A_Q_DIM:A_Q_DIM + A_KV_DIM].reshape(B, S, A_N_KV_HEADS, A_HEAD_DIM)
    v = qkv[..., A_Q_DIM + A_KV_DIM:].reshape(B, S, A_N_KV_HEADS, A_HEAD_DIM)
    q, k = rope(q, positions), rope(k, positions)
    o, _ = banded_attention(q, k, v, A_WINDOW - 1, sinks)
    return o.reshape(B, S, A_Q_DIM) @ w_o + b_o

def dilated_attention(q, k, v, window, dilation):
    B, S, H, Dh = q.shape
    Ls = S // dilation

    def to_sub(t):
        return t.reshape(B, Ls, dilation, H, Dh).transpose(0, 2, 1, 3, 4).reshape(B * dilation, Ls, H, Dh)

    o, lse = banded_attention(to_sub(q), to_sub(k), to_sub(v), window // dilation)
    o = o.reshape(B, dilation, Ls, H, Dh).transpose(0, 2, 1, 3, 4).reshape(B, S, H, Dh)
    lse = lse.reshape(B, dilation, Ls, H).transpose(0, 2, 1, 3).reshape(B, S, H)
    return o, lse

def dilated_mixer(h, positions, w_qkv, w_o):
    B, S, _ = h.shape
    GH = C_N_GROUPS * C_HEADS_PER_GROUP
    qkv = (h @ w_qkv).reshape(B, S, 3, GH, C_HEAD_DIM)
    q = rope(qkv[:, :, 0], positions).reshape(B, S, C_N_GROUPS, C_HEADS_PER_GROUP, C_HEAD_DIM)
    k = rope(qkv[:, :, 1], positions).reshape(B, S, C_N_GROUPS, C_HEADS_PER_GROUP, C_HEAD_DIM)
    v = qkv[:, :, 2].reshape(B, S, C_N_GROUPS, C_HEADS_PER_GROUP, C_HEAD_DIM)
    outs, lses = [], []
    for g, (window, dilation) in enumerate(C_PATTERNS):
        o, lse = dilated_attention(q[:, :, g], k[:, :, g], v[:, :, g], window, dilation)
        outs.append(o.astype(jnp.float32))
        lses.append(lse)
    wts = jax.nn.softmax(jnp.stack(lses, axis=0), axis=0)
    o = jnp.sum(wts[..., None] * jnp.stack(outs, axis=0), axis=0).astype(h.dtype)
    return o.reshape(B, S, C_HEADS_PER_GROUP * C_HEAD_DIM) @ w_o

def causal_depthwise_conv(x, w, b):
    C = x.shape[-1]
    y = lax.conv_general_dilated(x, w[:, None, :].astype(x.dtype), window_strides=(1,),
                                 padding=((SSM_CONV - 1, 0),),
                                 dimension_numbers=('NWC', 'WIO', 'NWC'),
                                 feature_group_count=C)
    return y + b

def ssd_chunked(xh, dt, A, Bm, Cm):
    b, S, H, P = xh.shape
    G, N, HG, Q = SSM_N_GROUPS, SSM_D_STATE, SSM_HEADS_PER_GROUP, SSM_CHUNK
    nc = S // Q
    x = (xh * dt[..., None]).reshape(b, nc, Q, G, HG, P)
    dA = (dt * A).reshape(b, nc, Q, G, HG).transpose(0, 1, 3, 4, 2)
    cs = jnp.cumsum(dA, axis=-1)
    Bc = Bm.reshape(b, nc, Q, G, N)
    Cc = Cm.reshape(b, nc, Q, G, N)
    tril = jnp.arange(Q)[:, None] >= jnp.arange(Q)[None, :]
    Lmat = jnp.exp(jnp.where(tril, cs[..., :, None] - cs[..., None, :], -jnp.inf))
    CB = jnp.einsum('bclgn,bcsgn->bcgls', Cc, Bc)
    y_diag = jnp.einsum('bcghls,bcsghp->bclghp', CB[:, :, :, None] * Lmat, x)
    decay_s = jnp.exp(cs[..., -1:] - cs)
    states = jnp.einsum('bclgn,bcghl,bclghp->bcghpn', Bc, decay_s, x)
    chunk_decay = jnp.exp(cs[..., -1])

    def step(state, inp):
        st, dec = inp
        return state * dec[..., None, None] + st, state

    init = jnp.zeros((b, G, HG, P, N), jnp.float32)
    _, prev = lax.scan(step, init, (jnp.moveaxis(states, 1, 0), jnp.moveaxis(chunk_decay, 1, 0)))
    prev = jnp.moveaxis(prev, 0, 1)
    y_off = jnp.einsum('bclgn,bcghpn,bcghl->bclghp', Cc, prev, jnp.exp(cs))
    return (y_diag + y_off).reshape(b, S, H, P)

def mamba2_mixer(h, in_w, conv_w, conv_b, dt_bias, a_log, d_skip, norm_w, out_w):
    B, S, _ = h.shape
    zxbcdt = h @ in_w
    z = zxbcdt[..., :SSM_D_INNER]
    xbc = zxbcdt[..., SSM_D_INNER:SSM_D_INNER + SSM_CONV_DIM]
    dt = zxbcdt[..., SSM_D_INNER + SSM_CONV_DIM:]
    xbc = jax.nn.silu(causal_depthwise_conv(xbc, conv_w, conv_b)).astype(jnp.float32)
    xs = xbc[..., :SSM_D_INNER].reshape(B, S, SSM_N_HEADS, SSM_HEAD_DIM)
    Bm = xbc[..., SSM_D_INNER:SSM_D_INNER + SSM_BC_DIM].reshape(B, S, SSM_N_GROUPS, SSM_D_STATE)
    Cm = xbc[..., SSM_D_INNER + SSM_BC_DIM:].reshape(B, S, SSM_N_GROUPS, SSM_D_STATE)
    dt = jax.nn.softplus(dt.astype(jnp.float32) + dt_bias.astype(jnp.float32))
    A = -jnp.exp(a_log.astype(jnp.float32))
    y = ssd_chunked(xs, dt, A, Bm, Cm) + d_skip.astype(jnp.float32)[:, None] * xs
    g = (y.reshape(B, S, SSM_D_INNER) * jax.nn.silu(z.astype(jnp.float32)))
    g = g.reshape(B, S, SSM_N_GROUPS, SSM_D_INNER // SSM_N_GROUPS)
    g = g * lax.rsqrt(jnp.mean(g * g, axis=-1, keepdims=True) + NORM_EPS)
    g = g.reshape(B, S, SSM_D_INNER) * norm_w.astype(jnp.float32)
    return g.astype(h.dtype) @ out_w

def sqrelu_mlp(h, w_up, w_down):
    u = jax.nn.relu(h @ w_up)
    return (u * u) @ w_down

def setup_inputs(seed: int = 0) -> dict:
    key = jax.random.key(seed)
    ks = jax.random.split(key, 24)
    f32 = jnp.float32
    res_scale = (2.0 * DEPTH) ** -0.5

    def nrm(k, shape, scale):
        return jax.random.normal(k, shape, f32) * scale

    x = jax.random.normal(ks[0], (BATCH, SEQ, D_MODEL), f32)
    offs = jax.random.randint(ks[1], (BATCH, 1), 0, 4096, dtype=jnp.int32)
    positions = offs + jnp.arange(SEQ, dtype=jnp.int32)[None, :]
    norm_mix_w = 1.0 + nrm(ks[2], (DEPTH, D_MODEL), 0.02)
    norm_mlp_w = 1.0 + nrm(ks[3], (DEPTH, D_MODEL), 0.02)
    a_w_qkv = nrm(ks[4], (N_A, D_MODEL, A_Q_DIM + 2 * A_KV_DIM), D_MODEL ** -0.5)
    a_b_qkv = nrm(ks[5], (N_A, A_Q_DIM + 2 * A_KV_DIM), 0.02)
    a_sinks = nrm(ks[6], (N_A, A_N_HEADS), 0.5)
    a_w_o = nrm(ks[7], (N_A, A_Q_DIM, D_MODEL), A_Q_DIM ** -0.5 * res_scale)
    a_b_o = nrm(ks[8], (N_A, D_MODEL), 0.02)
    b_in_w = nrm(ks[9], (N_B, D_MODEL, SSM_IN_DIM), D_MODEL ** -0.5)
    b_conv_w = nrm(ks[10], (N_B, SSM_CONV, SSM_CONV_DIM), SSM_CONV ** -0.5)
    b_conv_b = nrm(ks[11], (N_B, SSM_CONV_DIM), 0.02)
    dt0 = jnp.exp(jax.random.uniform(ks[12], (N_B, SSM_N_HEADS), f32, math.log(1e-3), math.log(1e-1)))
    b_dt_bias = dt0 + jnp.log(-jnp.expm1(-dt0))
    b_a_log = jnp.log(jax.random.uniform(ks[13], (N_B, SSM_N_HEADS), f32, 1.0, 16.0))
    b_d = 1.0 + nrm(ks[14], (N_B, SSM_N_HEADS), 0.02)
    b_norm_w = 1.0 + nrm(ks[15], (N_B, SSM_D_INNER), 0.02)
    b_out_w = nrm(ks[16], (N_B, SSM_D_INNER, D_MODEL), SSM_D_INNER ** -0.5 * res_scale)
    c_w_qkv = nrm(ks[17], (N_C, D_MODEL, C_QKV_DIM), D_MODEL ** -0.5)
    c_w_o = nrm(ks[18], (N_C, C_HEADS_PER_GROUP * C_HEAD_DIM, D_MODEL),
                (C_HEADS_PER_GROUP * C_HEAD_DIM) ** -0.5 * res_scale)
    mlp_w_up = nrm(ks[19], (DEPTH, D_MODEL, D_FF), D_MODEL ** -0.5)
    mlp_w_down = nrm(ks[20], (DEPTH, D_FF, D_MODEL), D_FF ** -0.5 * res_scale)
    final_norm_w = 1.0 + nrm(ks[21], (D_MODEL,), 0.02)
    return {"x": x, "positions": positions, "norm_mix_w": norm_mix_w, "norm_mlp_w": norm_mlp_w,
            "a_w_qkv": a_w_qkv, "a_b_qkv": a_b_qkv, "a_sinks": a_sinks, "a_w_o": a_w_o, "a_b_o": a_b_o,
            "b_in_w": b_in_w, "b_conv_w": b_conv_w, "b_conv_b": b_conv_b, "b_dt_bias": b_dt_bias,
            "b_a_log": b_a_log, "b_d": b_d, "b_norm_w": b_norm_w, "b_out_w": b_out_w,
            "c_w_qkv": c_w_qkv, "c_w_o": c_w_o, "mlp_w_up": mlp_w_up, "mlp_w_down": mlp_w_down,
            "final_norm_w": final_norm_w}

def reference(x, positions, norm_mix_w, norm_mlp_w, a_w_qkv, a_b_qkv, a_sinks, a_w_o, a_b_o,
              b_in_w, b_conv_w, b_conv_b, b_dt_bias, b_a_log, b_d, b_norm_w, b_out_w,
              c_w_qkv, c_w_o, mlp_w_up, mlp_w_down, final_norm_w):
    h = x
    for i in range(DEPTH):
        kind, j = i % N_MIXERS, i // N_MIXERS
        u = rmsnorm(h, norm_mix_w[i])
        if kind == 0:
            mix = swa_sink_mixer(u, positions, a_w_qkv[j], a_b_qkv[j], a_sinks[j], a_w_o[j], a_b_o[j])
        elif kind == 1:
            mix = mamba2_mixer(u, b_in_w[j], b_conv_w[j], b_conv_b[j], b_dt_bias[j], b_a_log[j],
                               b_d[j], b_norm_w[j], b_out_w[j])
        else:
            mix = dilated_mixer(u, positions, c_w_qkv[j], c_w_o[j])
        h = h + mix
        u = rmsnorm(h, norm_mlp_w[i])
        h = h + sqrelu_mlp(u, mlp_w_up[i], mlp_w_down[i])
    return rmsnorm(h, final_norm_w)


_drawn_inputs = setup_inputs


def setup_inputs(seed=0):
    import zlib

    import numpy as np

    out = dict(_drawn_inputs(seed))
    spreads = {}
    factors = {'norm_mix_w': 5.289,
     'norm_mlp_w': 3.349,
     'a_b_qkv': 5.512,
     'a_sinks': 8.0,
     'b_conv_b': 6.253,
     'b_d': 8.0,
     'b_norm_w': 8.0,
     'final_norm_w': 2.757}
    for name, (base, spread) in spreads.items():
        noise = np.random.default_rng([zlib.crc32(name.encode()), seed]).standard_normal(out[name].shape)
        drawn = base * np.exp(spread * noise) if base else spread * noise
        out[name] = __import__('jax').numpy.asarray(drawn.astype(out[name].dtype))
    for name, factor in factors.items():
        out[name] = (out[name] * factor).astype(out[name].dtype)
    return out
```

```python
from contextlib import ExitStack

import numpy as np

import concourse.bass as bass
from concourse import mybir

F32 = mybir.dt.float32
F32R = mybir.dt.float32r
BF16 = mybir.dt.bfloat16
I32 = mybir.dt.int32
ALU = mybir.AluOpType
ACT = mybir.ActivationFunctionType

P = 128
SEQ = 256
NT = SEQ // P
D = 1024
KT = D // P
DEPTH = 4
D_FF = 4 * D
HD = 64
HALF = HD // 2
EPS = 1e-5
ATT_SCALE = HD ** -0.5
BIG = 1e30

A_HEADS, A_KV = 16, 2
A_Q = A_HEADS * HD
A_QKV = A_Q + 2 * A_KV * HD
A_WINDOW = 128

INNER = 2 * D
SSM_HEADS = INNER // HD
GROUPS = 8
HPG = SSM_HEADS // GROUPS
GW = HPG * HD
TAPS = 4
BC = GROUPS * P
CONV = INNER + 2 * BC
CT_ALL = CONV // P
CT_X = INNER // P

C_GROUPS, C_HEADS = 3, 16
C_PATTERNS = ((128, 1), (512, 4), (2048, 16))
QUAD = 4
QUADS = A_HEADS // QUAD
QW = QUAD * HD

SMALL_LOADS = 7
CHUNK = 2048
RAW, RING = 2, 4
LEAD = RING - 1

A_BLOCKS = A_QKV // 256
MLP_STEPS, MLP_PER = 4, 8
PARTS = []
for layer in range(DEPTH):
    if layer % 3 == 0:
        PARTS += [(layer, "qkv", A_BLOCKS), (layer, "o", 4)]
    elif layer % 3 == 1:
        PARTS += [(layer, "xbc", 16), (layer, "dt", 1), (layer, "z", 8), (layer, "out", 8)]
    else:
        PARTS += [(layer, "qkv", 9 * QUADS), (layer, "o", 4)]
    PARTS += [(layer, "mlp", MLP_STEPS * MLP_PER)]
FIRST = {}
N_CHUNKS = 0
for _layer, _name, _n in PARTS:
    FIRST[_layer, _name] = N_CHUNKS
    N_CHUNKS += _n


def number(names, start=1):
    return {name: n for n, name in enumerate(names, start)}


T_STAGES = []
for layer in range(DEPTH):
    T_STAGES += [((layer, "norm"), KT), ((layer, "mix"), 2 * KT if layer % 3 == 1 else KT), ((layer, "mlp"), KT)]
T_FIRST, _n = {}, 0
for _name, _k in T_STAGES:
    T_FIRST[_name] = _n
    _n += _k // 2

NORMS = number([(layer, w) for layer in range(DEPTH) for w in ("norm", "mlp")] + ["final"], 0)
H_END, _n = {}, 0
for layer in range(DEPTH):
    for _what, _adds in (("mix", 4 if layer % 3 == 1 else 4 * QUADS), ("mlp", 4)):
        _n += _adds
        H_END[layer, _what] = _n

A_ORDER = [("kv", A_Q)] + [("q", n * QW) for n in range(4)]
C_ORDER = [("q", 0), ("k", 0), ("q", 1), ("k", 1), ("q", 2), ("k", 2), ("v", 0), ("v", 1), ("v", 2)]


def is_rotated(layer, b):
    return layer % 3 == 0 or C_ORDER[b % 9][0] != "v"


ROPE_NO, V_NO = {}, {}
UNIT0, HEAD0, QUAD0 = {}, {}, {}
for layer in (0, 2, 3):
    for b in range(A_BLOCKS if layer % 3 == 0 else 9 * QUADS):
        if is_rotated(layer, b):
            ROPE_NO[layer, b] = len(ROPE_NO)
        else:
            V_NO[layer, b] = len(V_NO)
for _m, layer in enumerate((0, 2, 3)):
    UNIT0[layer], HEAD0[layer], QUAD0[layer] = (0, 16, 64)[_m], 16 * _m, QUADS * _m


def order(layer):
    out = []
    if layer % 3 == 0:
        beside = {(2, 3): [0], (3, 0): [1], (3, 1): [2], (3, 2): [3], (3, 3): [4, 5],
                  (4, 0): [6], (4, 1): [7], (4, 3): [8, 9]}
        for b in range(A_BLOCKS):
            for m in range(4):
                out.append(("piece", b, m))
                if m == 0 and b:
                    out.append(("block", b - 1))
                if m == 3 and b:
                    out.append(("tq", b - 1))
                out += [("event", 0, e) for e in beside.get((b, m), [])]
        out += [("outputs", 0), ("event", 0, 10), ("event", 0, 11), ("mix", 0), ("block", 4)]
        o_beside = {(0, 1): [12], (0, 2): [13], (0, 3): [14], (1, 0): [15], (1, 1): [16], (1, 2): [17], (1, 3): [18],
                    (2, 0): [19], (2, 1): [20]}
        for q in range(QUADS):
            for m in range(4):
                out.append(("opiece", q, m))
                if (q, m) == (0, 1):
                    out.append(("tq", 4))
                out += [("event", 0, e) for e in o_beside.get((q, m), [])]
                if m == 1 and q < 3:
                    out.append(("outputs", q + 1))
            if q < 3:
                out.append(("mix", q + 1))
    else:
        for q in range(QUADS):
            for j in range(9):
                b = 9 * q + j
                for m in range(4):
                    out.append(("piece", b, m))
                    if m == 0 and b:
                        out.append(("block", b - 1))
                    if m == 1 and j == 0 and q >= 2:
                        out.append(("outputs", q - 2))
                    if m == 3 and b and is_rotated(layer, b - 1):
                        out.append(("tq", b - 1))
                    if m == 3 and j == 0 and q >= 2:
                        out.append(("mix", q - 2))
                    if q:
                        p = 4 * j + m
                        out += [("event", q - 1, e) for e in range(p * C_EVENTS // 36, (p + 1) * C_EVENTS // 36)]
        for q in range(3):
            for m in range(4):
                out.append(("opiece", q, m))
                if (q, m) == (0, 0):
                    out += [("block", 9 * QUADS - 1), ("outputs", 2)]
                if (q, m) == (0, 3):
                    out.append(("mix", 2))
                p = 4 * q + m
                out += [("event", 3, e) for e in range(p * C_EVENTS // 12, (p + 1) * C_EVENTS // 12)]
        out += [("outputs", 3), ("mix", 3)] + [("opiece", 3, m) for m in range(4)]
    return out


A_LEAD, C_LEAD = 3, 5
C_EVENTS = C_LEAD + QUAD * C_GROUPS + 2


def event_units(layer, q, e):
    lead, n, first = (A_LEAD, A_HEADS, 0) if layer % 3 == 0 else (C_LEAD, QUAD * C_GROUPS, QUAD * C_GROUPS * q)
    scores, turn, values = e, e - lead, e - lead - 2
    return [first + u if 0 <= u < n else None for u in (scores, turn, values)]


XS = 17408
NW = XS + NT * D
ARENA = 20480
COLS = 14336
M_R, M_SQ = 0, 2048
AT_P, AT_S = 0, 512
AT_ROT = 1024
AT_PT = 2048
AT_MASK = AT_PT + 3 * 384
AT_SM = AT_MASK + 3 * 384
AT_QKV = AT_SM + 3 * 1152
A_QT = AT_QKV
A_KT = A_QT + 2048
A_V = A_KT + 512
A_BIAS = A_V + 256
A_BO = A_BIAS + A_QKV
A_TMP = A_BO + D
assert A_TMP + 512 <= COLS
C_QT = AT_QKV
C_KT = C_QT + 2 * 1536
C_V = C_KT + 2 * 1536
assert C_V + 2 * 1536 <= XS
C_DIST = XS
R_FREQ = COLS + 4 * P
R_ARG = R_FREQ + 4 * HALF
assert R_ARG + 2 * HD <= XS
B_Z = 0
B_XC = 4096
B_G = B_XC
B_BT = B_XC + CT_X * SEQ
B_CT = B_BT + GROUPS * SEQ
B_XTOK = 12288
B_PAD = B_XTOK
B_ACC = B_PAD + 4 * 2 * 260
B_NW = B_XTOK
B_RL = 16384
B_E = B_RL + 512
B_XDEC = B_E + 1024
B_ST = B_XDEC + 512
B_XD = B_ST + 512
B_TMP = B_XD + 512
B_BTOK = B_TMP + 256
B_CBM = B_BTOK + 128
B_JUNK = B_CBM + 256
assert B_JUNK + 256 <= ARENA


def trunk(nc, x, positions, norm_mix_w, norm_mlp_w, a_w_qkv, a_b_qkv, a_sinks, a_w_o, a_b_o,
          b_in_w, b_conv_w, b_conv_b, b_dt_bias, b_a_log, b_d, b_norm_w, b_out_w,
          c_w_qkv, c_w_o, mlp_w_up, mlp_w_down, final_norm_w, rope_freq, out):
    ctx = ExitStack()
    with ctx:
        def sb(name, shape, dt=F32):
            return ctx.enter_context(nc.sbuf_tensor(name, shape, dt))

        def sem(name):
            return ctx.enter_context(nc.semaphore(name))

        raw = sb("raw", [P, RAW, CHUNK])
        w_hi = sb("w_hi", [P, RING, CHUNK], F32R)
        w_lo = sb("w_lo", [P, RING, CHUNK], F32R)
        xt = sb("xt", [P, 2, 2 * KT, SEQ], F32R)
        h = sb("h", [P, NT, D])
        ar = sb("arena", [P, ARENA])
        ident = sb("ident", [P, P])
        tril = sb("tril", [P, P])
        strict = sb("strict", [P, P])
        ones = sb("ones", [P, P])
        zero16 = sb("zero16", [P, P], BF16)
        cosr = sb("cosr", [P, NT, HD])
        sinr = sb("sinr", [P, NT, HD])
        pos_f = sb("pos_f", [P, NT])
        ssq = sb("ssq", [P, NT])
        var = sb("var", [P, NT])
        rstd = sb("rstd", [P, NT])
        mhalf = sb("mhalf", [P, 16])
        sinks = sb("sinks", [P, A_HEADS])
        nsinks = sb("nsinks", [P, A_HEADS])
        negmax = sb("negmax", [P, C_GROUPS, NT, A_HEADS])
        den = sb("den", [P, NT, A_HEADS])
        rden = sb("rden", [P, NT, A_HEADS])
        esk = sb("esk", [P, NT, A_HEADS])
        convw = sb("convw", [P, TAPS, CT_ALL])
        convb = sb("convb", [P, CT_ALL])
        dtb = sb("dtb", [P, SSM_HEADS])
        alog = sb("alog", [P, SSM_HEADS])
        dskip = sb("dskip", [P, SSM_HEADS])
        dt = sb("dt", [P, NT, SSM_HEADS])
        dt_t = sb("dt_t", [P, NT, SSM_HEADS])
        dt_u = sb("dt_u", [P, NT, SSM_HEADS])
        da = sb("da", [P, NT, SSM_HEADS])
        decay = sb("decay", [P, SSM_HEADS])
        ecs = sb("ecs", [P, SSM_HEADS])
        gss = sb("gss", [P, NT, GROUPS])
        grs = sb("grs", [P, NT, GROUPS])
        bank = [ctx.enter_context(nc.psum_tensor(f"bank{n}", [P, 512], F32)) for n in range(8)]

        def v(off, *dims):
            n = int(np.prod(dims))
            a = ar[:, off:off + n]
            if len(dims) == 1:
                return a
            names = "abcd"[:len(dims)]
            return a.rearrange(f"p ({' '.join(names)}) -> p {' '.join(names)}",
                               **{k: d for k, d in zip(names[1:], dims[1:])})

        xs = v(XS, NT, D)
        convw_rows, convb_rows = v(COLS, P), v(COLS + P, P)[0:CT_ALL, :]
        pos_rows, pos_rows_f = v(COLS + 2 * P, P)[0:NT, :].bitcast(I32), v(COLS + 3 * P, P)[0:NT, :]
        nw = v(NW, D)

        raw_in = [sem(f"raw_in{n}") for n in range(RAW)]
        hi_done, lo_done, chunk_done = sem("hi_done"), sem("lo_done"), sem("chunk_done")
        in_h, in_small, in_nw, in_bias, in_sink, in_gw = (sem(n) for n in ("in_h", "in_small", "in_nw", "in_bias", "in_sink", "in_gw"))
        pool_const, dist_made, cols_done, rope_arg, rope_tab, vec_const = (sem(n) for n in ("pool_const", "dist_made", "cols_done", "rope_arg", "rope_tab", "vec_const"))
        ssq_done, rstd_done, var_done, xs_done = sem("ssq_done"), sem("rstd_done"), sem("var_done"), sem("xs_done")
        t_done, xhi_done, xlo_done = sem("t_done"), sem("xhi_done"), sem("xlo_done")
        h_done = sem("h_done")
        relu_done, sq_done, uhi_done, ulo_done = sem("relu_done"), sem("sq_done"), sem("uhi_done"), sem("ulo_done")
        biased, rope_mul, roped, qt_done, qt_out, v_out, bo_added, wo_done, tile_done = (sem(n) for n in ("biased", "rope_mul", "roped", "qt_done", "qt_out", "v_out", "bo_added", "wo_done", "tile_done"))
        sc_done, sm_done, pr_done, pt_done, pt_out, pv_done = (sem(n) for n in ("sc_done", "sm_done", "pr_done", "pt_done", "pt_out", "pv_done"))
        esk_arg, esk_done, o_out = sem("esk_arg"), sem("esk_done"), sem("o_out")
        pad_done, conv_step, conv_out = (sem(n) for n in ("pad_done", "conv_step", "conv_out"))
        dt_pre, dt_e, dt_ln, dt_done, cs_done, cs_dec, cs_exp, dec_done = (sem(n) for n in ("dt_pre", "dt_e", "dt_ln", "dt_done", "cs_done", "cs_dec", "cs_exp", "dec_done"))
        xt_done, xtok_out_a, xtok_out_v, z_out = sem("xt_done"), sem("xtok_out_a"), sem("xtok_out_v"), sem("z_out")
        rl_done, xd_done, xdec_done, cb_done, cbm_done, seg_done, e_done, m_done = (sem(n) for n in ("rl_done", "xd_done", "xdec_done", "cb_done", "cbm_done", "seg_done", "e_done", "m_done"))
        btok_out, st_done, st_out, y_done, y_out, gate_done, gss_done, grs_done, gvar_done, ycomb, gn_done = (sem(n) for n in ("btok_out", "st_done", "st_out", "y_done", "y_out", "gate_done", "gss_done", "grs_done", "gvar_done", "ycomb", "gn_done"))
        out_done, chain = sem("out_done"), sem("chain")

        block = ctx.enter_context(nc.Block())

        def k_view(w):
            return w.rearrange("(k p) n -> p k n", p=P)

        def obank(l, n):
            return (n + (A_BLOCKS if l % 3 == 0 else 9 * QUADS)) % 2

        def of(n, i, per):
            return n if i is None else i * per + n

        @block.sync
        def _(sp):
            sp.dma_start(h[:, :, :], x[0].rearrange("(t p) d -> p t d", p=P)).then_inc(in_h, 16)

            def load(c, src, kts, i=None, per=0):
                if c >= RAW:
                    sp.wait_ge(lo_done, of(c - RAW + 1, i, per))
                n = kts * src.shape[-1]
                dst = raw[:, c % RAW, 0:n].rearrange("p (k n) -> p k n", k=kts)
                sp.dma_start(dst, src).then_inc(raw_in[c % RAW], 16)

            def mlp(l, steps, i=None, step0=0):
                wu, wd = k_view(mlp_w_up[l]), k_view(mlp_w_down[l])
                c = FIRST[l, "mlp"] + step0 * MLP_PER
                for j in range(4):
                    at = of((step0 * 4 + j) * 256, i, 1024)
                    load(c + j, wu[:, :, bass.ds(at, 256)], KT, i, MLP_PER)
                for j in range(4):
                    at = of(step0 * 8 + j // 2 * 4, i, 8)
                    load(c + 4 + j, wd[:, bass.ds(at, 4), (j % 2) * 512:(j % 2 + 1) * 512], 4, i, MLP_PER)

            def o_chunks(l, w):
                for q in range(QUADS):
                    load(FIRST[l, "o"] + q, w[:, 2 * q:2 * q + 2, :], 2)

            for l in range(DEPTH):
                if l % 3 == 0:
                    w = k_view(a_w_qkv[l // 3])
                    for n, (_, col) in enumerate(A_ORDER):
                        load(FIRST[l, "qkv"] + n, w[:, :, col:col + QW], KT)
                    o_chunks(l, k_view(a_w_o[l // 3]))
                elif l % 3 == 1:
                    w = k_view(b_in_w[0])
                    with sp.Fori(0, 4) as i:
                        for j in range(4):
                            load(FIRST[l, "xbc"] + j, w[:, :, bass.ds(i * 1024 + (INNER + j * 256), 256)], KT, i, 4)
                    load(FIRST[l, "dt"], w[:, :, INNER + CONV:INNER + CONV + SSM_HEADS], KT)
                    for nb in range(4):
                        for k in range(2):
                            load(FIRST[l, "z"] + 2 * nb + k, w[:, 4 * k:4 * k + 4, nb * 512:(nb + 1) * 512], 4)
                    w = k_view(b_out_w[0])
                    for k in range(4):
                        for nb in range(2):
                            load(FIRST[l, "out"] + 2 * k + nb, w[:, 4 * k:4 * k + 4, nb * 512:(nb + 1) * 512], 4)
                else:
                    w = k_view(c_w_qkv[0])
                    for q in range(QUADS):
                        for j, (kind, g) in enumerate(C_ORDER):
                            col = "qkv".index(kind) * C_GROUPS * D + g * D + q * QW
                            load(FIRST[l, "qkv"] + 9 * q + j, w[:, :, col:col + QW], KT)
                    o_chunks(l, k_view(c_w_o[0]))
                mlp(l, 1)
                with sp.Fori(0, MLP_STEPS - 1) as i:
                    mlp(l, MLP_STEPS, i, 1)
            for t in range(NT):
                sp.wait_ge(xs_done, NT * NORMS["final"] + t + 1)
                sp.dma_start(out[0, t * P:(t + 1) * P, :], xs[:, t, :]).then_inc(out_done, 16)
            sp.wait_ge(out_done, 16 * NT)

        @block.gpsimd
        def _(pool):
            chained = [0]

            def link(ins):
                chained[0] += 1
                ins.then_inc(pool_const, 1)
                pool.wait_ge(pool_const, chained[0])

            def row(w, n):
                return w.rearrange("(a n) -> a n", a=1).to_broadcast([P, n])

            pool.dma_start(nw, row(norm_mix_w[0], D)).then_inc(in_nw, 16)
            pool.dma_start(pos_rows, positions[0].rearrange("(t p) -> t p", p=P)).then_inc(in_small, 16)
            pool.dma_start(v(R_FREQ, HALF), row(rope_freq, HALF)).then_inc(in_small, 16)
            pool.dma_start(convb_rows, b_conv_b[0].rearrange("(c p) -> c p", p=P)).then_inc(in_small, 16)
            pool.dma_start(convw_rows, b_conv_w[0].rearrange("k (c p) -> (k c) p", p=P)).then_inc(in_small, 16)
            pool.dma_start(dtb[:, :], row(b_dt_bias[0], SSM_HEADS)).then_inc(in_small, 16)
            pool.dma_start(alog[:, :], row(b_a_log[0], SSM_HEADS)).then_inc(in_small, 16)
            pool.dma_start(dskip[:, :], row(b_d[0], SSM_HEADS)).then_inc(in_small, 16)

            link(pool.memset(ident[:, :], 0.0))
            link(pool.affine_select(out=ident[:, :], in_=ident[:, :], compare_op=ALU.not_equal, fill=1.0,
                                    base=0, pattern=[[-1, P]], channel_multiplier=1))
            pool.memset(tril[:, :], 1.0)
            pool.memset(ones[:, :], 1.0)
            pool.memset(mhalf[:, :], -0.5)
            link(pool.memset(strict[:, :], 1.0))
            pool.affine_select(out=tril[:, :], in_=tril[:, :], compare_op=ALU.is_ge, fill=0.0,
                               base=0, pattern=[[1, P]], channel_multiplier=-1)
            link(pool.affine_select(out=strict[:, :], in_=strict[:, :], compare_op=ALU.is_ge, fill=0.0,
                                    base=-1, pattern=[[-1, P]], channel_multiplier=1))

            def distances(dst):
                pool.iota(dst[:, 0:P], pattern=[[-1, P]], base=0, channel_multiplier=1)
                pool.iota(dst[:, P:3 * P], pattern=[[-1, 2 * P]], base=P, channel_multiplier=1).then_inc(dist_made, 1)

            def load_nw(w):
                pool.dma_start(nw, row(w, D)).then_inc(in_nw, 16)

            def rstds(name):
                n = NT * NORMS[name]
                for t in range(NT):
                    pool.wait_ge(ssq_done, n + t + 1)
                    pool.tensor_scalar(var[:, t:t + 1], ssq[:, t:t + 1], 1.0 / D, EPS, ALU.mult, ALU.add).then_inc(var_done, 1)
                    pool.wait_ge(var_done, n + t + 1)
                    pool.tensor_tensor(rstd[:, t:t + 1], var[:, t:t + 1], mhalf[:, 0:1], ALU.pow).then_inc(rstd_done, 1)

            for l in range(DEPTH):
                rstds((l, "norm"))
                if l % 3 == 0:
                    a = l // 3
                    if l:
                        pool.wait_ge(h_done, H_END[l - 1, "mlp"])
                    pool.dma_start(v(A_BIAS, A_QKV), row(a_b_qkv[a], A_QKV)).then_inc(in_bias, 16)
                    pool.dma_start(v(A_BO, D), row(a_b_o[a], D)).then_inc(in_sink, 16)
                    if l:
                        pool.wait_ge(o_out, QUADS)
                    pool.dma_start(sinks[:, :], row(a_sinks[a], A_HEADS)).then_inc(in_sink, 16)

                if l % 3 != 1:
                    pool.wait_ge(t_done, T_FIRST[l, "norm"] + KT // 2)
                    distances(v(C_DIST, 3 * P).bitcast(I32))

                def rotate_sum(b, width, dup=False):
                    n = ROPE_NO[l, b]
                    dst = v(AT_ROT + (n % 2) * 512, NT, 256)
                    p_, s_ = v(AT_P, NT, 256), v(AT_S, NT, 256)
                    for t in range(NT):
                        pool.wait_ge(rope_mul, NT * n + t + 1)
                        if t == 0 and n >= 2:
                            pool.wait_ge(qt_done, n - 1)
                        if dup:
                            for e in range(2):
                                o = dst[:, t, :].rearrange("p (g e d) -> p g e d", e=2, d=HD)[:, :, e, :]
                                ins = pool.tensor_tensor(o, p_[:, t, 0:width].rearrange("p (g d) -> p g d", d=HD),
                                                         s_[:, t, 0:width].rearrange("p (g d) -> p g d", d=HD), ALU.add)
                        else:
                            ins = pool.tensor_tensor(dst[:, t, :], p_[:, t, :], s_[:, t, :], ALU.add)
                        ins.then_inc(roped, 1)

                if l % 3 == 0:
                    for b in range(A_BLOCKS):
                        rotate_sum(b, A_KV * HD if b == 0 else QW, dup=b == 0)
                    pool.wait_ge(xs_done, NT * (NORMS[l, "norm"] + 1))
                    pool.wait_ge(in_sink, 32 * (a + 1))
                    for t in range(NT):
                        pool.tensor_tensor(h[:, t, :], h[:, t, :], v(A_BO, D), ALU.add).then_inc(bo_added, 1)
                elif l % 3 == 1:
                    pool.wait_ge(h_done, H_END[l - 1, "mlp"])
                    for n in range(4):
                        pool.memset(v(B_PAD + n * 520, 2, 260)[:, :, 0:3], 0.0).then_inc(pad_done, 1)
                    pool.memset(v(B_ACC, 1), 0.0).then_inc(conv_out, 1)
                    pool.wait_ge(dt_done, 2)
                    for u in range(2 * GROUPS):
                        g, c = u // 2, u % 2
                        if u >= 1:
                            pool.wait_ge(seg_done, u)
                        else:
                            pool.wait_ge(xs_done, NT * (NORMS[l, "norm"] + 1))
                        pool.tensor_tensor(v(B_RL, HPG, P),
                                           da[:, c, HPG * g:HPG * g + HPG].unsqueeze(2).to_broadcast([P, HPG, P]),
                                           tril[:, :].unsqueeze(1).to_broadcast([P, HPG, P]), ALU.mult).then_inc(rl_done, 1)
                        xg = v(B_XTOK, NT, INNER)[:, c, g * GW:(g + 1) * GW].rearrange("p (h d) -> p h d", d=HD)
                        pool.wait_ge(xtok_out_a, 4)
                        pool.wait_ge(xtok_out_v, 4)
                        if u >= 2:
                            pool.wait_ge(y_out, u - 1)
                        pool.tensor_tensor(v(B_XD + (u % 2) * 256, HPG, HD), xg,
                                           dskip[:, HPG * g:HPG * g + HPG].unsqueeze(2).to_broadcast([P, HPG, HD]), ALU.mult).then_inc(xd_done, 1)
                        if c == 0:
                            pool.wait_ge(dec_done, 1)
                            if g >= 2:
                                pool.wait_ge(st_done, 2 * (g - 2) + 1)
                            pool.tensor_tensor(v(B_XDEC + (g % 2) * 256, HPG, HD), xg,
                                               decay[:, HPG * g:HPG * g + HPG].unsqueeze(2).to_broadcast([P, HPG, HD]), ALU.mult).then_inc(xdec_done, 1)
                    pool.wait_ge(y_done, 2 * GROUPS)
                    pool.dma_start(v(B_NW, INNER), row(b_norm_w[0], INNER)).then_inc(in_gw, 16)
                    pool.wait_ge(gss_done, 2 * GROUPS)
                    pool.tensor_scalar(gss[:, :, :], gss[:, :, :], 1.0 / GW, EPS, ALU.mult, ALU.add).then_inc(gvar_done, 1)
                    pool.wait_ge(gvar_done, 1)
                    pool.tensor_tensor(grs[:, :, :], gss[:, :, :], mhalf[:, 0:16].rearrange("p (t g) -> p t g", t=NT), ALU.pow).then_inc(grs_done, 1)
                    pool.wait_ge(y_out, 2 * GROUPS)
                else:
                    for b in range(9 * QUADS):
                        if is_rotated(l, b):
                            rotate_sum(b, QW)
                pool.wait_ge(xs_done, NT * (NORMS[l, "norm"] + 1))
                load_nw(norm_mlp_w[l])
                rstds((l, "mlp"))
                pool.wait_ge(xs_done, NT * (NORMS[l, "mlp"] + 1))
                load_nw(norm_mix_w[l + 1] if l + 1 < DEPTH else final_norm_w)
            rstds("final")

        @block.scalar
        def _(act):
            def split(c, i=None, per=0, width=CHUNK):
                if c >= N_CHUNKS:
                    return
                if c == FIRST[1, "dt"]:
                    width = KT * SSM_HEADS
                use, per_use = c // RAW + 1, per // RAW
                act.wait_ge(raw_in[c % RAW], of(16 * use, i, 16 * per_use))
                if c >= RING:
                    act.wait_ge(chunk_done, of(c - RING + 1, i, per))
                act.activation(w_hi[:, c % RING, 0:width], raw[:, c % RAW, 0:width], ACT.Copy).then_inc(hi_done, 1)

            def norm(end):
                for t in range(NT):
                    if end:
                        act.wait_ge(h_done, end - 2 * (NT - 1 - t))
                    else:
                        act.wait_ge(in_h, 16)
                    act.activation(xs[:, t, :], h[:, t, :], ACT.Square, accum_out=ssq[:, t:t + 1]).then_inc(ssq_done, 1)

            def t_hi_norm(name):
                for n in range(4):
                    t, k = n // 2, n % 2 * 4
                    act.wait_ge(t_done, T_FIRST[name] + n + 1)
                    act.activation(xt[:, 0, k:k + 4, t * P:(t + 1) * P], bank[4 + n][:, :].rearrange("p (k n) -> p k n", k=4), ACT.Copy)\
                       .then_inc(xhi_done, 1)

            def t_hi(name, j, k, b):
                act.wait_ge(t_done, T_FIRST[name] + j + 1)
                act.activation(xt[:, 0, k:k + 2, :], bank[b][:, :].rearrange("p (k n) -> p k n", k=2), ACT.Copy).then_inc(xhi_done, 1)

            def steps(c, n):
                for k in range(n):
                    split(c + k + LEAD)

            def mlp(l, i=None, step0=0):
                c, u = FIRST[l, "mlp"] + step0 * MLP_PER, 16 * l + 4 * step0
                for j in range(MLP_PER):
                    if j in (1, 2, 3, 4):
                        k = j - 1
                        act.wait_ge(chunk_done, of(c + k + 1, i, MLP_PER))
                        act.activation(v(M_R, 4, 512)[:, k, :], bank[4 + k][:, :], ACT.Relu).then_inc(relu_done, 1)
                    split(c + j + LEAD, i, MLP_PER)
                    if j in (1, 2, 3, 4):
                        k = j - 1
                        act.wait_ge(sq_done, of(u + k + 1, i, 4))
                        act.activation(xt[:, 0, KT + 2 * k:KT + 2 * k + 2, :], v(M_SQ, 4, 2, SEQ)[:, k], ACT.Copy).then_inc(uhi_done, 1)

            def attention(l):
                ng = 1 if l % 3 == 0 else C_GROUPS
                u0, h0, w = UNIT0[l], HEAD0[l], 3 * P * ng
                slots = 4 if ng == 1 else 3
                sm = v(AT_SM, slots, w)
                c = FIRST[l, "qkv"]

                def exps(n):
                    act.wait_ge(sm_done, 2 * (u0 + (n + 1) * ng))
                    for b in range(NT):
                        at = slice(0, P * ng) if b == 0 else slice(P * ng, w)
                        act.activation(sm[:, n % slots, at], sm[:, n % slots, at], ACT.Exp, scale=-1.0,
                                       bias=negmax[:, ng - 1, b, n:n + 1], accum_out=den[:, b, n:n + 1]).then_inc(pr_done, 1)

                for step in order(l):
                    what, q, m = step[0], step[1], step[-1]
                    if what in ("piece", "opiece") and m == 0:
                        split((c if what == "piece" else FIRST[l, "o"]) + q + LEAD)
                    elif what == "block" and l == 0 and q == 0:
                            for t in range(NT):
                                act.wait_ge(rope_arg, 2 * t + 2)
                                src = v(R_ARG + t * HD, 2, HALF)
                                act.activation(cosr[:, t, 0:HALF], src[:, 0, :], ACT.Sin).then_inc(rope_tab, 1)
                                act.activation(sinr[:, t, HALF:HD], src[:, 1, :], ACT.Sin).then_inc(rope_tab, 1)
                    elif what == "block" and not is_rotated(l, q):
                        act.wait_ge(chunk_done, c + q + 1)
                        vv = v(C_V + q // 9 % 2 * 1536, NT, C_GROUPS, QW)[:, :, C_ORDER[q % 9][1], :]
                        act.activation(vv, bank[q % 2][:, :].rearrange("p (t n) -> p t n", t=NT), ACT.Copy).then_inc(v_out, 1)
                    elif what == "tq":
                        n = ROPE_NO[l, q]
                        act.wait_ge(qt_done, n + 1)
                        if l % 3 == 0:
                            dst = v(A_KT, 2, SEQ) if q == 0 else v(A_QT, 4, 2, SEQ)[:, q - 1]
                        else:
                            kind, g = C_ORDER[q % 9]
                            dst = v((C_QT if kind == "q" else C_KT) + q // 9 % 2 * 1536, C_GROUPS, 2, SEQ)[:, g]
                        act.activation(dst, bank[7][:, :].rearrange("p (k n) -> p k n", k=2), ACT.Copy).then_inc(qt_out, 1)
                    elif what == "mix":
                        t_hi((l, "mix"), q, KT + 2 * q, 7)
                    elif what == "event":
                        _, turn, _ = event_units(l, q, m)
                        if m == (1 if ng == 1 else 3):
                            exps(QUAD * q)
                        if turn is not None:
                            act.wait_ge(pt_done, u0 + turn + 1)
                            if turn >= 3:
                                act.wait_ge(pv_done, u0 + turn - 2)
                            act.activation(v(AT_PT + turn % 3 * 384, 384), bank[6][:, 0:3 * P], ACT.Copy).then_inc(pt_out, 1)
                            n = turn // ng
                            if ng == 1 and n % QUAD == QUAD - 1:
                                e = slice(n - QUAD + 1, n + 1)
                                act.wait_ge(esk_arg, QUADS * (l // 3) + n // QUAD + 1)
                                act.activation(esk[:, :, e], esk[:, :, e], ACT.Exp).then_inc(esk_done, 1)
                            if turn % ng == 0 and (n + 1 < A_HEADS if ng == 1 else n % QUAD < QUAD - 1):
                                exps(n + 1)

            for c in range(LEAD):
                split(c)
            adds = 0
            for l in range(DEPTH):
                norm(adds)
                t_hi_norm((l, "norm"))
                if l % 3 != 1:
                    attention(l)
                elif l % 3 == 1:
                    c = FIRST[l, "xbc"]
                    act.wait_ge(pad_done, 4)
                    act.wait_ge(vec_const, 3)
                    with act.Fori(0, 4) as i:
                        act.wait_ge(conv_out, of(1, i, 4))
                        for j in range(4):
                            split(c + j + LEAD, i, 4)
                            act.wait_ge(chunk_done, of(c + j + 1, i, 4))
                            for e in range(2):
                                ct = i * 8 + (2 * j + e)
                                act.activation(v(B_ACC + j * 512, 2, 256)[:, e, :], bank[4 + j][:, e * SEQ:(e + 1) * SEQ], ACT.Identity,
                                               scale=convw[:, 3, bass.ds(ct, 1)], bias=convb[:, bass.ds(ct, 1)])
                            act.activation(v(B_PAD + j * 520, 2, 260)[:, :, 3:259], bank[4 + j][:, :].rearrange("p (k n) -> p k n", k=2), ACT.Copy)\
                               .then_inc(pad_done, 1)
                            for k in ([j - 1] if j else []) + ([3] if j == 3 else []):
                                act.wait_ge(conv_step, of(6 * (k + 1), i, 24))
                                act.activation(ar[:, bass.ds(i * 2048 + (B_XC + k * 512), 512)], v(B_ACC + k * 512, 512), ACT.Silu)\
                                   .then_inc(conv_out, 1)
                    split(FIRST[l, "dt"] + LEAD)

                    def z_block(nb):
                        c = FIRST[l, "z"] + 2 * nb
                        split(c + LEAD)
                        split(c + 1 + LEAD)
                        act.wait_ge(chunk_done, c + 2)
                        for t in range(NT):
                            act.activation(v(B_Z, NT, INNER)[:, t, nb * 512:(nb + 1) * 512],
                                           bank[2 * ((nb + 1) % 2) + t][:, :], ACT.Silu).then_inc(z_out, 1)

                    z_block(0)
                    for n in range(1, 8, 2):
                        act.wait_ge(xt_done, n + 1)
                        act.activation(v(B_XTOK, 8, 512)[:, n, :], bank[4 + n % 4][:, :], ACT.Copy).then_inc(xtok_out_a, 1)
                    act.wait_ge(dt_pre, 2)
                    act.wait_ge(in_small, 16 * SMALL_LOADS)
                    act.activation(alog[:, :], alog[:, :], ACT.Exp).then_inc(dt_e, 1)
                    act.activation(dt_t[:, :, :], dt_t[:, :, :], ACT.Exp).then_inc(dt_e, 1)
                    act.wait_ge(dt_e, 2)
                    act.activation(dt_t[:, :, :], dt_t[:, :, :], ACT.Ln, bias=1.0).then_inc(dt_ln, 1)
                    z_block(1)
                    act.wait_ge(cs_done, 1)
                    act.activation(ecs[:, :], bank[5][:, 0:SSM_HEADS], ACT.Exp).then_inc(cs_exp, 1)
                    act.wait_ge(cs_dec, 2)
                    act.activation(decay[:, :], decay[:, :], ACT.Exp).then_inc(cs_exp, 1)
                    z_block(2)
                    z_block(3)
                    for u in range(2 * GROUPS + 2):
                        g, c = u // 2, u % 2
                        if u < 2 * GROUPS:
                            act.wait_ge(seg_done, u + 1)
                            if u >= 2:
                                act.wait_ge(y_done, u - 1)
                            act.activation(v(B_E + (u % 2) * 512, 512), bank[6 + u % 2][:, :], ACT.Exp).then_inc(e_done, 1)
                            if c == 1:
                                act.wait_ge(st_done, 2 * g + 1)
                                act.activation(v(B_ST + (g % 2) * 256, 256), bank[2][:, 0:256], ACT.Copy).then_inc(st_out, 1)
                        if u >= 2:
                            k = u - 2
                            act.wait_ge(gate_done, k + 1)
                            if k:
                                act.wait_ge(gss_done, k)
                            act.activation(v(B_JUNK, 256), v(B_G, NT, INNER)[:, k % 2, k // 2 * GW:(k // 2 + 1) * GW], ACT.Square,
                                           accum_out=gss[:, k % 2, k // 2:k // 2 + 1]).then_inc(gss_done, 1)
                    for j in range(KT):
                        t_hi((l, "mix"), j, 2 * j, 4 + j % 4)
                    steps(FIRST[l, "out"], 8)
                norm(H_END[l, "mix"])
                t_hi_norm((l, "mlp"))
                mlp(l)
                last = l == DEPTH - 1
                with act.Fori(0, MLP_STEPS - 1 - last) as i:
                    mlp(l, i, 1)
                if last:
                    mlp(l, None, MLP_STEPS - 1)
                adds = H_END[l, "mlp"]
            norm(adds)

        @block.vector
        def _(dve):
            chained = [0]

            def link(ins):
                chained[0] += 1
                ins.then_inc(chain, 1)
                dve.wait_ge(chain, chained[0])

            def split(c, i=None, per=0, width=CHUNK):
                if c >= N_CHUNKS:
                    return
                if c == FIRST[1, "dt"]:
                    width = KT * SSM_HEADS
                dve.wait_ge(hi_done, of(c + 1, i, per))
                if c >= RING:
                    dve.wait_ge(chunk_done, of(c - RING + 1, i, per))
                dve.tensor_tensor(w_lo[:, c % RING, 0:width], raw[:, c % RAW, 0:width],
                                  w_hi[:, c % RING, 0:width].bitcast(F32), ALU.subtract).then_inc(lo_done, 1)

            def steps(c, n):
                for k in range(n):
                    split(c + k + LEAD)

            def norm(name):
                n = NORMS[name]
                dve.wait_ge(in_nw, 16 * (n + 1))
                for t in range(NT):
                    dve.wait_ge(rstd_done, NT * n + t + 1)
                    dve.scalar_tensor_tensor(out=xs[:, t, :], in0=h[:, t, :], scalar=rstd[:, t:t + 1], in1=nw,
                                             op0=ALU.mult, op1=ALU.mult).then_inc(xs_done, 1)

            def t_lo_norm(name):
                for n in range(4):
                    t, k = n // 2, n % 2 * 4
                    dve.wait_ge(xhi_done, T_FIRST[name] + n + 1)
                    dve.tensor_tensor(xt[:, 1, k:k + 4, t * P:(t + 1) * P], bank[4 + n][:, :].rearrange("p (k n) -> p k n", k=4),
                                      xt[:, 0, k:k + 4, t * P:(t + 1) * P].bitcast(F32), ALU.subtract).then_inc(xlo_done, 1)

            def t_lo(name, j, k, b):
                dve.wait_ge(xhi_done, T_FIRST[name] + j + 1)
                dve.tensor_tensor(xt[:, 1, k:k + 2, :], bank[b][:, :].rearrange("p (k n) -> p k n", k=2),
                                  xt[:, 0, k:k + 2, :].bitcast(F32), ALU.subtract).then_inc(xlo_done, 1)

            def add(dst, b):
                dve.tensor_tensor(dst, bank[b][:, :], dst, ALU.add).then_inc(h_done, 1)

            def residual(c_end, tile):
                for t in range(NT):
                    for nb in range(2):
                        if t == 0:
                            dve.wait_ge(tile_done, tile)
                        else:
                            dve.wait_ge(chunk_done, c_end - 1 + nb)
                        add(h[:, t, nb * 512:(nb + 1) * 512], 2 * nb + t)

            def mlp(l, i=None, step0=0):
                c, u = FIRST[l, "mlp"] + step0 * MLP_PER, 16 * l + 4 * step0
                for j in range(MLP_PER):
                    if j in (1, 2, 3, 4):
                        k = j - 1
                        dve.wait_ge(relu_done, of(u + k + 1, i, 4))
                        dve.tensor_tensor(v(M_SQ, 4, 512)[:, k, :], v(M_R, 4, 512)[:, k, :], v(M_R, 4, 512)[:, k, :], ALU.mult).then_inc(sq_done, 1)
                    split(c + j + LEAD, i, MLP_PER)
                    if j in (1, 2, 3, 4):
                        k = j - 1
                        dve.wait_ge(uhi_done, of(u + k + 1, i, 4))
                        dve.tensor_tensor(xt[:, 1, KT + 2 * k:KT + 2 * k + 2, :], v(M_SQ, 4, 2, SEQ)[:, k],
                                          xt[:, 0, KT + 2 * k:KT + 2 * k + 2, :].bitcast(F32), ALU.subtract).then_inc(ulo_done, 1)

            def masks(l, dst, patterns):
                dist = v(C_DIST, 3 * P).bitcast(I32)
                f, m, r = v(C_DIST + 384, 3 * P), v(C_DIST + 768, 3 * P), v(C_DIST + 1152, 3 * P)
                dve.wait_ge(dist_made, 1 + [0, 2, 3].index(l))
                link(dve.tensor_copy(f, dist))
                for n, (window, dilation) in enumerate(patterns):
                    o = dst[:, n * 384:(n + 1) * 384]
                    link(dve.tensor_scalar(m, f, float(window), None, ALU.is_le))
                    link(dve.scalar_tensor_tensor(out=o, in0=f, scalar=0.0, in1=m, op0=ALU.is_ge, op1=ALU.mult))
                    if dilation > 1:
                        link(dve.tensor_scalar(r.bitcast(I32), dist, dilation - 1, None, ALU.bitwise_and))
                        link(dve.tensor_copy(m, r.bitcast(I32)))
                        link(dve.scalar_tensor_tensor(out=o, in0=m, scalar=0.0, in1=o, op0=ALU.is_equal, op1=ALU.mult))
                    link(dve.tensor_scalar(o, o, -1.0, BIG, ALU.add, ALU.mult))

            def rotate(n, width, src):
                nh = width // HD
                for t in range(NT):
                    if n:
                        dve.wait_ge(roped, NT * (n - 1) + t + 1)
                    x_ = src(t).rearrange("p (h d) -> p h d", d=HD)
                    p_ = v(AT_P, NT, 256)[:, t, 0:width].rearrange("p (h d) -> p h d", d=HD)
                    s_ = v(AT_S, NT, 256)[:, t, 0:width].rearrange("p (h d) -> p h d", d=HD)
                    dve.tensor_tensor(p_, x_, cosr[:, t, :].unsqueeze(1).to_broadcast([P, nh, HD]), ALU.mult)
                    dve.tensor_tensor(s_[:, :, 0:HALF], x_[:, :, HALF:HD], sinr[:, t, 0:HALF].unsqueeze(1).to_broadcast([P, nh, HALF]), ALU.mult)
                    dve.tensor_tensor(s_[:, :, HALF:HD], x_[:, :, 0:HALF], sinr[:, t, HALF:HD].unsqueeze(1).to_broadcast([P, nh, HALF]), ALU.mult)\
                       .then_inc(rope_mul, 1)

            def attention(l):
                ng = 1 if l % 3 == 0 else C_GROUPS
                u0, h0, w = UNIT0[l], HEAD0[l], 3 * P * ng
                slots = 4 if ng == 1 else 3
                sm, mask = v(AT_SM, slots, w), v(AT_MASK, 3, 384)
                c, a = FIRST[l, "qkv"], l // 3
                bias, tmp, vv = v(A_BIAS, A_QKV), v(A_TMP, NT, QW), v(A_V, NT, P)

                def scores(u):
                    n, g = u // ng, u % ng
                    dve.wait_ge(sc_done, u0 + u + 1)
                    if g == 0 and n >= slots:
                        dve.wait_ge(pt_done, u0 + (n - slots + 1) * ng)
                    for b in range(NT):
                        k = P * (b + 1)
                        at = P * g if b == 0 else P * ng + 2 * P * g
                        src = slice(0, P) if b == 0 else slice(P, 3 * P)
                        if g:
                            dve.wait_ge(sm_done, 2 * (u0 + u) + b - 1)
                            first = negmax[:, g - 1, b, n:n + 1]
                        else:
                            first = nsinks[:, n:n + 1] if ng == 1 else 3e38
                        dve.tensor_tensor_reduce(out=sm[:, n % slots, at:at + k], in0=bank[4 + u % 2][:, src],
                                                 in1=mask[:, g, src], scale=-ATT_SCALE, scalar=first,
                                                 op0=ALU.add, op1=ALU.min,
                                                 accum_out=negmax[:, g, b, n:n + 1]).then_inc(sm_done, 1)
                    if ng == 1 and n % QUAD == QUAD - 1:
                        e = slice(n - QUAD + 1, n + 1)
                        dve.wait_ge(sm_done, 2 * (u0 + u + 1))
                        for b in range(NT):
                            ins = dve.tensor_tensor(esk[:, b, e], sinks[:, e], negmax[:, 0, b, e], ALU.add)
                        ins.then_inc(esk_arg, 1)

                def outputs(q):
                    e = slice(QUAD * q, QUAD * (q + 1))
                    dve.wait_ge(pr_done, 2 * (h0 + QUAD * (q + 1)))
                    src = den
                    if ng == 1:
                        dve.wait_ge(esk_done, QUADS * a + q + 1)
                        link(dve.tensor_tensor(rden[:, :, e], den[:, :, e], esk[:, :, e], ALU.add))
                        src = rden
                    link(dve.reciprocal(rden[:, :, e], src[:, :, e]))
                    dve.wait_ge(pv_done, u0 + QUAD * (q + 1) * ng)
                    for b in range(NT):
                        ins = dve.tensor_tensor(xs[:, b, q * QW:(q + 1) * QW].rearrange("p (h d) -> p h d", d=HD),
                                                bank[2 + q % 2][:, b * QW:(b + 1) * QW].rearrange("p (h d) -> p h d", d=HD),
                                                rden[:, b, e].unsqueeze(2).to_broadcast([P, QUAD, HD]), ALU.mult)
                    ins.then_inc(o_out, 1)

                for step in order(l):
                    what, q, m = step[0], step[1], step[-1]
                    if what == "piece" and m == 1:
                        split(c + q + LEAD)
                    elif what == "opiece":
                        if m == 1:
                            split(FIRST[l, "o"] + q + LEAD)
                        t, nb, n = m // 2, m % 2, 4 * q + m
                        if m < 3:
                            dve.wait_ge(wo_done, 3 * (QUAD0[l] + q) + m + 1)
                        else:
                            dve.wait_ge(chunk_done, FIRST[l, "o"] + q + 1)
                        if n >= 4:
                            dve.wait_ge(h_done, H_END[l, "mix"] - 4 * QUADS + n - 3)
                        elif n == 0 and ng == 1:
                            dve.wait_ge(bo_added, NT * (a + 1))
                        add(h[:, t, nb * 512:(nb + 1) * 512], obank(l, n))
                    elif what == "block" and is_rotated(l, q):
                        n = ROPE_NO[l, q]
                        dve.wait_ge(chunk_done, c + q + 1)
                        ps = bank[q % 2][:, :].rearrange("p (t n) -> p t n", t=NT)
                        if ng > 1:
                            rotate(n, QW, lambda t: ps[:, t, :])
                            continue
                        k, width = A_ORDER[q][1], P if q == 0 else QW
                        if n:
                            dve.wait_ge(rope_mul, NT * n)
                        for t in range(NT):
                            if q == 0:
                                dve.tensor_tensor(vv[:, t, :], ps[:, t, P:QW], bias[:, k + P:k + QW], ALU.add)
                            dve.tensor_tensor(tmp[:, t, 0:width], ps[:, t, 0:width], bias[:, k:k + width], ALU.add).then_inc(biased, 1)
                        dve.wait_ge(biased, NT * (A_BLOCKS * a + q + 1))
                        if n == 0:
                            rotary_tables()
                        rotate(n, width, lambda t: tmp[:, t, 0:width])
                    elif what == "outputs":
                        outputs(q)
                    elif what == "mix":
                        t_lo((l, "mix"), q, KT + 2 * q, 7)
                    elif what == "event":
                        u, _, _ = event_units(l, q, m)
                        if u is not None:
                            scores(u)

            def rotary_tables():
                freq, ang, kk = v(R_FREQ, HALF), v(R_FREQ + HALF, HALF), v(R_FREQ + 2 * HALF, HALF)
                two_pi = [6.28125, 0.0019350051879882812, 3.0198689e-07]
                dve.wait_ge(cols_done, 1)
                dve.tensor_copy(convw[:, :, :], bank[3][:, 0:P].rearrange("p (k c) -> p k c", k=TAPS)).then_inc(vec_const, 1)
                dve.tensor_copy(convb[:, :], bank[3][:, P:P + CT_ALL]).then_inc(vec_const, 1)
                dve.tensor_copy(pos_f[:, :], bank[3][:, 2 * P:2 * P + NT]).then_inc(vec_const, 1)
                dve.wait_ge(vec_const, 4)
                for t in range(NT):
                    link(dve.tensor_scalar(ang, freq, pos_f[:, t:t + 1], None, ALU.mult))
                    for e, turn in ((0, 0.25), (1, 0.0)):
                        arg = v(R_ARG + t * HD, 2, HALF)[:, e, :]
                        link(dve.tensor_scalar(kk, ang, 0.5 / np.pi, turn, ALU.mult, ALU.add))
                        link(dve.tensor_scalar(kk, kk, 12582912.0, 12582912.0, ALU.add, ALU.subtract))
                        link(dve.scalar_tensor_tensor(out=arg, in0=kk, scalar=-two_pi[0], in1=ang, op0=ALU.mult, op1=ALU.add))
                        for part in two_pi[1:]:
                            link(dve.scalar_tensor_tensor(out=arg, in0=kk, scalar=-part, in1=arg, op0=ALU.mult, op1=ALU.add))
                        if turn:
                            link(dve.tensor_scalar(arg, arg, np.pi / 2, None, ALU.add))
                        dve.tensor_scalar(arg, arg, 3.1415925, -3.1415925, ALU.min, ALU.max).then_inc(rope_arg, 1)
                for t in range(NT):
                    dve.wait_ge(rope_tab, 2 * t + 2)
                    dve.tensor_copy(cosr[:, t, HALF:HD], cosr[:, t, 0:HALF])
                    link(dve.tensor_scalar(sinr[:, t, 0:HALF], sinr[:, t, HALF:HD], -1.0, None, ALU.mult))

            for c in range(LEAD):
                split(c)
            for l in range(DEPTH):
                norm((l, "norm"))
                t_lo_norm((l, "norm"))
                if l == 0:
                    dve.wait_ge(in_small, 16 * SMALL_LOADS)
                    link(dve.memset(zero16[:, :], 0.0))
                    dve.tensor_copy(pos_rows_f, pos_rows).then_inc(vec_const, 1)
                if l % 3 == 0:
                    a = l // 3
                    masks(l, v(AT_MASK, 384), [(A_WINDOW - 1, 1)])
                    dve.wait_ge(in_bias, 16 * (a + 1))
                    dve.wait_ge(in_sink, 32 * (a + 1))
                    link(dve.tensor_scalar(nsinks[:, :], sinks[:, :], -1.0, None, ALU.mult))
                    attention(l)
                elif l % 3 == 1:
                    c = FIRST[l, "xbc"]
                    dve.wait_ge(in_small, 16 * SMALL_LOADS)
                    with dve.Fori(0, 4) as i:
                        for j in range(4):
                            split(c + j + LEAD, i, 4)
                            for n in range(6):
                                k, e = 2 - n // 2, n % 2
                                if n < 2:
                                    dve.wait_ge(pad_done, of(4 + j + 1, i, 4))
                                else:
                                    dve.wait_ge(conv_step, of(6 * j + n - 1, i, 24))
                                acc = v(B_ACC + j * 512, 2, 256)[:, e, :]
                                dve.scalar_tensor_tensor(out=acc, in0=v(B_PAD + j * 520, 2, 260)[:, e, k:k + 256],
                                                         scalar=convw[:, k, bass.ds(i * 8 + (2 * j + e), 1)], in1=acc,
                                                         op0=ALU.mult, op1=ALU.add).then_inc(conv_step, 1)
                    c = FIRST[l, "dt"]
                    split(c + LEAD)
                    dve.wait_ge(chunk_done, c + 1)
                    for t in range(NT):
                        link(dve.tensor_tensor(dt_u[:, t, :], bank[t][:, 0:SSM_HEADS], dtb[:, :], ALU.add))
                        dve.scalar_tensor_tensor(out=dt_t[:, t, :], in0=dt_u[:, t, :], scalar=-1.0, in1=dt_u[:, t, :],
                                                 op0=ALU.mult, op1=ALU.min).then_inc(dt_pre, 1)
                    c = FIRST[l, "z"]
                    steps(c, 2)
                    for n in range(0, 8, 2):
                        dve.wait_ge(xt_done, n + 1)
                        dve.tensor_copy(v(B_XTOK, 8, 512)[:, n, :], bank[4 + n % 4][:, :]).then_inc(xtok_out_v, 1)
                    dve.wait_ge(dt_ln, 1)
                    link(dve.scalar_tensor_tensor(out=dt[:, :, :], in0=dt_u[:, :, :], scalar=0.0, in1=dt_t[:, :, :],
                                                  op0=ALU.max, op1=ALU.add))
                    for t in range(NT):
                        dve.scalar_tensor_tensor(out=da[:, t, :], in0=dt[:, t, :], scalar=-1.0, in1=alog[:, :],
                                                 op0=ALU.mult, op1=ALU.mult).then_inc(dt_done, 1)
                    steps(c + 2, 2)
                    dve.wait_ge(cs_done, 1)
                    dve.tensor_copy(dt_u[:, 0, :], bank[4][:, 0:SSM_HEADS]).then_inc(cs_dec, 1)
                    dve.wait_ge(cs_dec, 1)
                    dve.tensor_tensor(decay[:, :], bank[4][:, 32:64], dt_u[:, 0, :], ALU.subtract).then_inc(cs_dec, 1)
                    steps(c + 4, 2)
                    dve.wait_ge(cs_exp, 2)
                    dve.tensor_tensor(decay[:, :], decay[:, :], dt[:, 0, :], ALU.mult).then_inc(dec_done, 1)
                    steps(c + 6, 2)
                    y_all, z_all = v(B_G, NT, INNER), v(B_Z, NT, INNER)

                    def combine(u):
                        g, c = u // 2, u % 2
                        y = y_all[:, c, g * GW:(g + 1) * GW]
                        dve.wait_ge(y_done, u + 1)
                        dve.wait_ge(xd_done, u + 1)
                        ins = dve.tensor_tensor(y, bank[u % 2][:, 0:GW], v(B_XD + (u % 2) * 256, 256), ALU.add)
                        ins.then_inc(y_out, 1)
                        if c == 1:
                            dve.wait_ge(st_done, 2 * g + 2)
                            dve.tensor_tensor(v(B_TMP, HPG, HD), bank[3][:, 0:GW].rearrange("p (h d) -> p h d", d=HD),
                                              ecs[:, HPG * g:HPG * g + HPG].unsqueeze(2).to_broadcast([P, HPG, HD]), ALU.mult).then_inc(ycomb, 1)
                            dve.wait_ge(ycomb, g + 1)
                            dve.wait_ge(y_out, u + 1)
                            link(dve.tensor_tensor(y, y, v(B_TMP, 256), ALU.add))
                        else:
                            dve.wait_ge(y_out, u + 1)
                        dve.tensor_tensor(y, y, z_all[:, c, g * GW:(g + 1) * GW], ALU.mult).then_inc(gate_done, 1)

                    dve.wait_ge(z_out, 8)
                    for u in range(2 * GROUPS + 1):
                        g, c = u // 2, u % 2
                        if u < 2 * GROUPS:
                            cbm = v(B_CBM + c * P, P)
                            dve.wait_ge(cb_done, u + 1)
                            if c == 0:
                                if g:
                                    dve.wait_ge(st_done, 2 * g - 1)
                                dve.tensor_copy(v(B_BTOK, P), bank[4][:, P:2 * P]).then_inc(btok_out, 1)
                            dve.tensor_tensor(cbm, bank[4 + c][:, 0:P], tril[:, :], ALU.mult).then_inc(cbm_done, 1)
                            dve.wait_ge(cbm_done, u + 1)
                            dve.wait_ge(e_done, u + 1)
                            for k in range(HPG):
                                e = v(B_E + c * 512, HPG, P)[:, k, :]
                                ins = dve.scalar_tensor_tensor(out=e, in0=e, scalar=dt[:, c, HPG * g + k:HPG * g + k + 1], in1=cbm,
                                                               op0=ALU.mult, op1=ALU.mult)
                            ins.then_inc(m_done, 1)
                        if u:
                            combine(u - 1)
                    dve.wait_ge(in_gw, 16)
                    dve.wait_ge(grs_done, 1)
                    for g in range(GROUPS):
                        for t in range(NT):
                            y = y_all[:, t, g * GW:(g + 1) * GW]
                            dve.scalar_tensor_tensor(out=y, in0=y, scalar=grs[:, t, g:g + 1], in1=v(B_NW, INNER)[:, g * GW:(g + 1) * GW],
                                                     op0=ALU.mult, op1=ALU.mult).then_inc(gn_done, 1)
                    for j in range(KT):
                        t_lo((l, "mix"), j, 2 * j, 4 + j % 4)
                    c = FIRST[l, "out"]
                    steps(c, 8)
                    residual(c + 8, 2 * MLP_STEPS + 4)
                else:
                    masks(l, v(AT_MASK, 3 * 384), C_PATTERNS)
                    attention(l)
                norm((l, "mlp"))
                t_lo_norm((l, "mlp"))
                mlp(l)
                last = l == DEPTH - 1
                with dve.Fori(0, MLP_STEPS - 1 - last) as i:
                    mlp(l, i, 1)
                if last:
                    mlp(l, None, MLP_STEPS - 1)
                residual(FIRST[l, "mlp"] + MLP_STEPS * MLP_PER, 2 * MLP_STEPS * (l + 1) + 4 * (l >= 1))
            norm("final")

        @block.tensor
        def _(pe):
            def mm(dst, lhs, rhs, start, stop):
                return pe.matmul(dst, lhs, rhs, start=start, stop=stop)

            def transposed(name, j, src, b):
                for t in range(NT):
                    for k in range(2):
                        ins = pe.transpose(bank[b][:, k * SEQ + t * P:k * SEQ + (t + 1) * P],
                                           src[:, t, (2 * j + k) * P:(2 * j + k + 1) * P], ident[:, :])
                ins.then_inc(t_done, 1)

            def transposed_norm(name, t):
                pe.wait_ge(xs_done, NT * NORMS[name] + t + 1)
                for n in range(2):
                    for k in range(4):
                        ins = pe.transpose(bank[4 + 2 * t + n][:, k * P:(k + 1) * P], xs[:, t, (4 * n + k) * P:(4 * n + k + 1) * P], ident[:, :])
                    ins.then_inc(t_done, 1)

            def tokens(c, kts, width, b, k0=0, first=True, last=True, g0=None, i=None, per=0, check=True):
                pe.wait_ge(lo_done, of(c + 1, i, per))
                hi = w_hi[:, c % RING, 0:kts * width].rearrange("p (k n) -> p k n", k=kts)
                lo = w_lo[:, c % RING, 0:kts * width].rearrange("p (k n) -> p k n", k=kts)
                for t in range(NT):
                    dst = bank[b + t][:, 0:width]
                    for k in range(kts):
                        if g0 is not None and k % 2 == 0 and t == 0:
                            pe.wait_ge(xlo_done, g0 + (k0 + k) // 2 + 1)
                        for n, (s, w) in enumerate(((0, hi), (1, hi), (0, lo))):
                            ins = pe.matmul(dst, xt[:, s, k0 + k, t * P:(t + 1) * P], w[:, k, :],
                                            start=first and k == 0 and n == 0,
                                            stop=last and k == kts - 1 and n == 2, skip_group_check=not check)
                ins.then_inc(chunk_done, 1)

            def features(c, b, i=None, per=0, by_tile=None):
                pe.wait_ge(lo_done, of(c + 1, i, per))
                hi = w_hi[:, c % RING, :].rearrange("p (k n) -> p k n", k=KT)
                lo = w_lo[:, c % RING, :].rearrange("p (k n) -> p k n", k=KT)
                for t in range(NT if by_tile else 1):
                    if by_tile and t:
                        transposed_norm(by_tile, t)
                    cols = slice(t * P, (t + 1) * P) if by_tile else slice(0, SEQ)
                    for e in range(2):
                        for k in range(KT):
                            if by_tile and e == 0 and k % 4 == 0:
                                pe.wait_ge(xlo_done, T_FIRST[by_tile] + 2 * t + k // 4 + 1)
                            for n, (s, w) in enumerate(((0, hi), (1, hi), (0, lo))):
                                ins = pe.matmul(bank[b][:, e * SEQ:(e + 1) * SEQ][:, cols], w[:, k, e * P:(e + 1) * P], xt[:, s, k, cols],
                                                start=k == 0 and n == 0, stop=k == KT - 1 and n == 2)
                ins.then_inc(chunk_done, 1)

            def two_chunks(c, k0, first, last, i=None, per=0):
                pe.wait_ge(lo_done, of(c + 2, i, per))
                for t in range(NT):
                    for nb in range(2):
                        hi = w_hi[:, (c + nb) % RING, :].rearrange("p (k n) -> p k n", k=4)
                        lo = w_lo[:, (c + nb) % RING, :].rearrange("p (k n) -> p k n", k=4)
                        for k in range(4):
                            for n, (s, w) in enumerate(((0, hi), (1, hi), (0, lo))):
                                ins = pe.matmul(bank[2 * nb + t][:, :], xt[:, s, k0 + k, t * P:(t + 1) * P], w[:, k, :],
                                                start=first and k == 0 and n == 0, stop=last and k == 3 and n == 2, skip_group_check=True)
                        if t:
                            ins.then_inc(chunk_done, 1)
                    if t == 0:
                        ins.then_inc(tile_done, 1)

            def attention(l):
                ng = 1 if l % 3 == 0 else C_GROUPS
                u0, h0, w = UNIT0[l], HEAD0[l], 3 * P * ng
                slots = 4 if ng == 1 else 3
                sm = v(AT_SM, slots, w)
                c, a, name = FIRST[l, "qkv"], l // 3, (l, "norm")

                def q_of(n, g):
                    at = slice(64 * (n % 2), 64 * (n % 2) + 64)
                    if ng == 1:
                        return v(A_QT, 8, SEQ)[at, n // 2, :]
                    return v(C_QT + n // QUAD % 2 * 1536, C_GROUPS, 2, SEQ)[at, g, n % QUAD // 2, :]

                def k_of(n, g):
                    at = slice(64 * (n % 2), 64 * (n % 2) + 64)
                    if ng == 1:
                        return v(A_KT, 2, SEQ)[at, n // 8, :]
                    return v(C_KT + n // QUAD % 2 * 1536, C_GROUPS, 2, SEQ)[at, g, n % QUAD // 2, :]

                def v_of(n, g, t):
                    if ng == 1:
                        return v(A_V, NT, P)[:, t, n // 8 * HD:n // 8 * HD + HD]
                    k = n % QUAD * HD
                    return v(C_V + n // QUAD % 2 * 1536, NT, C_GROUPS, QW)[:, t, g, k:k + HD]

                def scores(u):
                    n, g = u // ng, u % ng
                    if n % QUAD == 0 and g == 0:
                        last = 1 + n // QUAD if ng == 1 else 9 * (n // QUAD) + 5
                        pe.wait_ge(qt_out, ROPE_NO[l, last] + 1)
                    if u >= 2:
                        pe.wait_ge(sm_done, 2 * (u0 + u - 1))
                    q, k = q_of(n, g), k_of(n, g)
                    mm(bank[4 + u % 2][:, 0:P], q[:, 0:P], k[:, 0:P], True, True)
                    mm(bank[4 + u % 2][:, P:3 * P], q[:, P:2 * P], k[:, 0:2 * P], True, True).then_inc(sc_done, 1)

                def turn(u):
                    n, g = u // ng, u % ng
                    if g == 0:
                        pe.wait_ge(pr_done, 2 * (h0 + n + 1))
                    if u:
                        pe.wait_ge(pt_out, u0 + u)
                    for m, at in enumerate((P * g, P * ng + 2 * P * g, P * ng + 2 * P * g + P)):
                        ins = pe.transpose(bank[6][:, m * P:(m + 1) * P], sm[:, n % slots, at:at + P], ident[:, :])
                    ins.then_inc(pt_done, 1)

                def values(u):
                    n, g = u // ng, u % ng
                    q = n // QUAD
                    b = bank[2 + q % 2]
                    if n % QUAD == 0 and g == 0:
                        if q >= 2:
                            pe.wait_ge(o_out, QUAD0[l] + q - 1)
                        if ng > 1:
                            pe.wait_ge(v_out, V_NO[l, 9 * q + 8] + 1)
                        for e in range(2):
                            pe.matmul(b[:, e * QW:(e + 1) * QW], zero16[:, :], tril[:, :].bitcast(BF16), start=e == 0, stop=False,
                                      skip_group_check=True)
                    pe.wait_ge(pt_out, u0 + u + 1)
                    pt = v(AT_PT + u % 3 * 384, 3, P)
                    at = n % QUAD * HD
                    for m, (o, t) in enumerate(((at, 0), (QW + at, 0), (QW + at, 1))):
                        ins = pe.matmul(b[:, o:o + HD], pt[:, m, :], v_of(n, g, t), start=False, stop=False, skip_group_check=True)
                    ins.then_inc(pv_done, 1)

                def bank_free(b):
                    if ng == 1:
                        pe.wait_ge(biased, NT * (A_BLOCKS * a + b + 1))
                    elif is_rotated(l, b):
                        pe.wait_ge(rope_mul, NT * (ROPE_NO[l, b] + 1))
                    else:
                        pe.wait_ge(v_out, V_NO[l, b] + 1)

                blocks = A_BLOCKS if ng == 1 else 9 * QUADS
                bank7 = [None]
                for step in order(l):
                    what, q, m = step[0], step[1], step[-1]
                    if what == "piece":
                        t, k0 = m // 2, 4 * (m % 2)
                        if m == 0:
                            pe.wait_ge(lo_done, c + q + 1)
                            if q >= 2:
                                bank_free(q - 2)
                        if q == 0:
                            if m == 2:
                                transposed_norm(name, 1)
                            pe.wait_ge(xlo_done, T_FIRST[name] + m + 1)
                        hi = w_hi[:, (c + q) % RING, :].rearrange("p (k n) -> p k n", k=KT)
                        lo = w_lo[:, (c + q) % RING, :].rearrange("p (k n) -> p k n", k=KT)
                        for k in range(k0, k0 + 4):
                            for n, (s, w_) in enumerate(((0, hi), (1, hi), (0, lo))):
                                ins = pe.matmul(bank[q % 2][:, t * QW:(t + 1) * QW], xt[:, s, k, t * P:(t + 1) * P], w_[:, k, :],
                                                start=k == 0 and n == 0, stop=k == KT - 1 and n == 2)
                        if m == 3:
                            ins.then_inc(chunk_done, 1)
                            if l == 0 and q == 0:
                                columns()
                    elif what == "opiece":
                        t, nb, n = m // 2, m % 2, 4 * q + m
                        cc = FIRST[l, "o"] + q
                        if m == 0:
                            pe.wait_ge(lo_done, cc + 1)
                            pe.wait_ge(xlo_done, T_FIRST[l, "mix"] + q + 1)
                        if n < 2:
                            bank_free(blocks - 2 + n)
                        else:
                            pe.wait_ge(h_done, H_END[l, "mix"] - 4 * QUADS + n - 1)
                        hi = w_hi[:, cc % RING, :].rearrange("p (k n) -> p k n", k=2)
                        lo = w_lo[:, cc % RING, :].rearrange("p (k n) -> p k n", k=2)
                        for k in range(2):
                            for e, (s, w_) in enumerate(((0, hi), (1, hi), (0, lo))):
                                ins = pe.matmul(bank[obank(l, n)][:, :], xt[:, s, KT + 2 * q + k, t * P:(t + 1) * P],
                                                w_[:, k, nb * 512:(nb + 1) * 512], start=k == 0 and e == 0, stop=k == 1 and e == 2)
                        ins.then_inc(wo_done if m < 3 else chunk_done, 1)
                    elif what == "tq":
                        n = ROPE_NO[l, q]
                        if bank7[0]:
                            pe.wait_ge(*bank7[0])
                        pe.wait_ge(roped, NT * (n + 1))
                        src = v(AT_ROT + (n % 2) * 512, NT, 256)
                        for k in range(2):
                            for t in range(NT):
                                ins = pe.transpose(bank[7][:, k * SEQ + t * P:k * SEQ + (t + 1) * P], src[:, t, k * P:(k + 1) * P], ident[:, :])
                        ins.then_inc(qt_done, 1)
                        bank7[0] = (qt_out, n + 1)
                    elif what == "mix":
                        if bank7[0]:
                            pe.wait_ge(*bank7[0])
                        pe.wait_ge(o_out, QUAD0[l] + q + 1)
                        transposed((l, "mix"), q, xs, 7)
                        bank7[0] = (xlo_done, T_FIRST[l, "mix"] + q + 1)
                    elif what == "event":
                        s_, t_, v_ = event_units(l, q, m)
                        if t_ is not None:
                            turn(t_)
                        if s_ is not None:
                            scores(s_)
                        if v_ is not None:
                            values(v_)

            def columns():
                pe.wait_ge(in_small, 16 * SMALL_LOADS)
                pe.wait_ge(vec_const, 1)
                pe.transpose(bank[3][:, 0:P], convw_rows, ident[:, :])
                pe.transpose(bank[3][:, P:P + CT_ALL], convb_rows, ident[0:CT_ALL, 0:CT_ALL])
                pe.transpose(bank[3][:, 2 * P:2 * P + NT], pos_rows_f, ident[0:NT, 0:NT]).then_inc(cols_done, 1)

            pe.wait_ge(pool_const, 4)
            for l in range(DEPTH):
                transposed_norm((l, "norm"), 0)
                if l % 3 != 1:
                    attention(l)
                else:
                    c = FIRST[l, "xbc"]
                    transposed_norm((l, "norm"), 1)
                    pe.wait_ge(xlo_done, T_FIRST[l, "norm"] + 4)
                    with pe.Fori(0, 4) as i:
                        for j in range(4):
                            pe.wait_ge(pad_done, of(j + 1, i, 4))
                            features(c + j, 4 + j, i, 4)
                    tokens(FIRST[l, "dt"], KT, SSM_HEADS, 0)
                    c = FIRST[l, "z"]

                    def z_block(nb):
                        b = 2 * ((nb + 1) % 2)
                        if nb == 1:
                            pe.wait_ge(dt_pre, 2)
                        if nb >= 2:
                            pe.wait_ge(z_out, 2 * (nb - 1))
                        for k in range(2):
                            tokens(c + 2 * nb + k, 4, 512, b, 4 * k, first=k == 0, last=k == 1)

                    z_block(0)
                    xc = v(B_XC, CT_ALL, SEQ)
                    pe.wait_ge(conv_out, 17)
                    for n in range(8):
                        t, q = n // 4, n % 4
                        if n >= 4 and n % 2:
                            pe.wait_ge(xtok_out_a, (n - 4) // 2 + 1)
                        if n >= 4 and n % 2 == 0:
                            pe.wait_ge(xtok_out_v, (n - 4) // 2 + 1)
                        for k in range(4):
                            ins = pe.transpose(bank[4 + n % 4][:, k * P:(k + 1) * P], xc[:, 4 * q + k, t * P:(t + 1) * P], ident[:, :])
                        ins.then_inc(xt_done, 1)
                    z_block(1)
                    pe.wait_ge(dt_done, 2)
                    pe.wait_ge(xtok_out_v, 4)
                    pe.wait_ge(xtok_out_a, 4)
                    mm(bank[4][:, 0:32], tril[:, :], da[:, 0, :], True, True)
                    mm(bank[4][:, 32:64], ones[:, :], da[:, 0, :], True, True)
                    mm(bank[5][:, 0:32], tril[:, :], da[:, 1, :], True, True).then_inc(cs_done, 1)
                    z_block(2)
                    z_block(3)
                    bt, ct = v(B_BT, GROUPS, SEQ), v(B_CT, GROUPS, SEQ)
                    xtok = v(B_XTOK, NT, INNER)
                    pe.wait_ge(cs_exp, 2)
                    pe.wait_ge(cs_dec, 2)
                    pe.wait_ge(z_out, 8)

                    def first_stage(u):
                        g, c = u // 2, u % 2
                        tok = slice(c * P, (c + 1) * P)
                        if u >= 2:
                            pe.wait_ge(cbm_done, u - 1)
                        if c == 0:
                            if g >= 1:
                                pe.wait_ge(btok_out, g)
                            pe.transpose(bank[4][:, P:2 * P], bt[:, g, 0:P], ident[:, :])
                        mm(bank[4 + c][:, 0:P], bt[:, g, tok], ct[:, g, tok], True, True).then_inc(cb_done, 1)
                        pe.wait_ge(rl_done, u + 1)
                        if u >= 2:
                            pe.wait_ge(e_done, u - 1)
                        mm(bank[6 + u % 2][:, :], strict[:, :], v(B_RL, 512), True, True).then_inc(seg_done, 1)

                    def second_stage(u):
                        g, c = u // 2, u % 2
                        if u >= 2:
                            pe.wait_ge(y_out, u - 1)
                        pe.wait_ge(m_done, u + 1)
                        for k in range(HPG):
                            ins = mm(bank[u % 2][:, k * HD:(k + 1) * HD], v(B_E + c * 512, HPG, P)[:, k, :],
                                     xtok[:, c, g * GW + k * HD:g * GW + (k + 1) * HD], True, True)
                        ins.then_inc(y_done, 1)
                        if c == 0:
                            pe.wait_ge(btok_out, g + 1)
                            pe.wait_ge(xdec_done, g + 1)
                            if g:
                                pe.wait_ge(st_out, g)
                            mm(bank[2][:, 0:GW], v(B_BTOK, P), v(B_XDEC + (g % 2) * 256, 256), True, True).then_inc(st_done, 1)
                        else:
                            pe.wait_ge(st_out, g + 1)
                            if g:
                                pe.wait_ge(ycomb, g)
                            mm(bank[3][:, 0:GW], ct[:, g, P:2 * P], v(B_ST + (g % 2) * 256, 256), True, True).then_inc(st_done, 1)

                    first_stage(0)
                    for u in range(2 * GROUPS):
                        if u + 1 < 2 * GROUPS:
                            first_stage(u + 1)
                        second_stage(u)
                    for j in range(KT):
                        pe.wait_ge(gn_done, 2 * j + 2)
                        if j >= 4:
                            pe.wait_ge(xlo_done, T_FIRST[l, "mix"] + j - 3)
                        transposed((l, "mix"), j, v(B_G, NT, INNER), 4 + j % 4)
                    for k in range(4):
                        pe.wait_ge(xlo_done, T_FIRST[l, "mix"] + 2 * k + 2)
                        two_chunks(FIRST[l, "out"] + 2 * k, 4 * k, k == 0, k == 3)
                transposed_norm((l, "mlp"), 0)
                pe.wait_ge(h_done, H_END[l, "mix"])
                for b in range(4):
                    for e in range(2):
                        pe.matmul(bank[b][:, e * 256:(e + 1) * 256], zero16[:, :], tril[:, :].bitcast(BF16), start=e == 0, stop=False,
                                  skip_group_check=True)

                def mlp(i, step0):
                    c, u = FIRST[l, "mlp"] + step0 * MLP_PER, 16 * l + 4 * step0
                    for j in range(4):
                        features(c + j, 4 + j, i, MLP_PER, by_tile=(l, "mlp") if step0 == 0 and j == 0 else None)
                    for f in range(2):
                        pe.wait_ge(ulo_done, of(u + 2 * f + 2, i, 4))
                        two_chunks(c + 4 + 2 * f, KT + 4 * f, False, False, i, MLP_PER)

                last = l == DEPTH - 1
                mlp(None, 0)
                with pe.Fori(0, MLP_STEPS - 1 - last) as i:
                    mlp(i, 1)
                if last:
                    mlp(None, MLP_STEPS - 1)


_INS = ["x", "positions", "norm_mix_w", "norm_mlp_w", "a_w_qkv", "a_b_qkv", "a_sinks", "a_w_o", "a_b_o",
        "b_in_w", "b_conv_w", "b_conv_b", "b_dt_bias", "b_a_log", "b_d", "b_norm_w", "b_out_w",
        "c_w_qkv", "c_w_o", "mlp_w_up", "mlp_w_down", "final_norm_w"]


def kernel(**inputs):
    import numpy as _np
    import concourse.bacc as _bacc
    from concourse import mybir as _mybir
    from concourse.bass_utils import run_bass_kernel_spmd as _run

    nc = _bacc.Bacc("TRN2", target_bir_lowering=False, num_devices=1)
    arrays, args = {}, []

    def give(name, a):
        arrays[f"in_{name}"] = a
        args.append(nc.dram_tensor(f"in_{name}", a.shape, _mybir.dt.from_np(a.dtype), kind="ExternalInput").ap())

    for name in _INS:
        give(name, _np.ascontiguousarray(inputs[name]))
    give("rope_freq", (10000.0 ** (-_np.arange(HALF, dtype=_np.float32) / _np.float32(HALF))).astype(_np.float32))
    args.append(nc.dram_tensor("out", (1, SEQ, D), F32, kind="ExternalOutput").ap())
    trunk(nc, *args)
    r = _run(nc, [arrays], core_ids=[0])
    return r.results[0]["out"]
```

```python
from contextlib import ExitStack

import numpy as np

import concourse.bass as bass
from concourse import mybir

F32 = mybir.dt.float32
F32R = mybir.dt.float32r
BF16 = mybir.dt.bfloat16
I32 = mybir.dt.int32
ALU = mybir.AluOpType
ACT = mybir.ActivationFunctionType

P = 128
SEQ = 256
NT = SEQ // P
D = 1024
KT = D // P
DEPTH = 4
HD = 64
HALF = HD // 2
EPS = 1e-5
ATT_SCALE = HD ** -0.5
BIG = 1e30

A_HEADS, A_KV = 16, 2
A_Q = A_HEADS * HD
A_QKV = A_Q + 2 * A_KV * HD
A_WINDOW = 128

INNER = 2 * D
SSM_HEADS = INNER // HD
GROUPS = 8
HPG = SSM_HEADS // GROUPS
GW = HPG * HD
TAPS = 4
BC = GROUPS * P
CONV = INNER + 2 * BC
CT_ALL = CONV // P
CT_X = INNER // P

C_GROUPS = 3
C_PATTERNS = ((128, 1), (512, 4), (2048, 16))
QUAD = 4
QUADS = A_HEADS // QUAD
QW = QUAD * HD

SMALL_LOADS = 6
CHUNK = 2048
RAW, RING = 2, 4
LEAD = RING - 1

A_BLOCKS = A_QKV // 256
MLP_STEPS, MLP_PER = 4, 8
PARTS = []
for layer in range(DEPTH):
    if layer % 3 == 0:
        PARTS += [(layer, "qkv", A_BLOCKS), (layer, "o", 4)]
    elif layer % 3 == 1:
        PARTS += [(layer, "z0", 2), (layer, "dt", 1), (layer, "xbc", 16), (layer, "z", 6), (layer, "out", 8)]
    else:
        PARTS += [(layer, "qkv", 9 * QUADS), (layer, "o", 4)]
    PARTS += [(layer, "mlp", MLP_STEPS * MLP_PER)]
FIRST = {}
N_CHUNKS = 0
for _layer, _name, _n in PARTS:
    FIRST[_layer, _name] = N_CHUNKS
    N_CHUNKS += _n


def number(names, start):
    return {name: n for n, name in enumerate(names, start)}


T_STAGES = []
for layer in range(DEPTH):
    T_STAGES += [((layer, "norm"), KT), ((layer, "mix"), 2 * KT if layer % 3 == 1 else KT), ((layer, "mlp"), KT)]
T_FIRST, _n = {}, 0
for _name, _k in T_STAGES:
    T_FIRST[_name] = _n
    _n += _k // 2

NORMS = number([(layer, w) for layer in range(DEPTH) for w in ("norm", "mlp")] + ["final"], 0)
O_ADDS = 12
H_END, _n = {}, 0
for layer in range(DEPTH):
    for _what, _adds in (("mix", 4 if layer % 3 == 1 else O_ADDS), ("mlp", 4)):
        _n += _adds
        H_END[layer, _what] = _n

A_ORDER = [("kv", A_Q)] + [("q", n * QW) for n in range(4)]
C_ORDER = [("q", 0), ("k", 0), ("q", 1), ("k", 1), ("q", 2), ("k", 2), ("v", 0), ("v", 1), ("v", 2)]


def is_rotated(layer, b):
    return layer % 3 == 0 or C_ORDER[b % 9][0] != "v"


ROPE_NO, V_NO = {}, {}
UNIT0, HEAD0, QUAD0 = {}, {}, {}
for layer in (0, 2, 3):
    for b in range(A_BLOCKS if layer % 3 == 0 else 9 * QUADS):
        if is_rotated(layer, b):
            ROPE_NO[layer, b] = len(ROPE_NO)
        else:
            V_NO[layer, b] = len(V_NO)
for _m, layer in enumerate((0, 2, 3)):
    UNIT0[layer], HEAD0[layer], QUAD0[layer] = (0, 16, 64)[_m], 16 * _m, QUADS * _m


def order(layer):
    out = []

    def pieces(b, ms):
        return [("piece", b, m) for m in ms]

    blocks = A_BLOCKS if layer % 3 == 0 else 9 * QUADS
    out += pieces(0, (0, 1)) + [("split", 3)] + pieces(1, (0,)) + [("turn", 1)] + pieces(1, (1,)) + pieces(0, (2, 3)) + [("block", 0)]
    out += pieces(1, (2,)) + [("split", 4)] + pieces(1, (3,))
    if layer % 3 == 0:
        events = {(2, 3): [0, 1], (3, 0): [2], (3, 1): [3], (3, 2): [4], (3, 3): [5],
                  (4, 0): [6], (4, 1): [7], (4, 2): [8], (4, 3): [9]}
        for b in range(2, blocks):
            for m in range(4):
                out += pieces(b, (m,))
                if m == 0:
                    out.append(("block", b - 1))
                if m == 1:
                    out.append(("split", b + LEAD))
                if (b, m) == (2, 1):
                    out += [("tq", 0), ("mask", 0)]
                if m == 2:
                    out.append(("tq", b - 1))
                out += [("event", 0, e) for e in events.get((b, m), [])]
        out[-1:-1] = [("outputs", 0)]
        out += [("block", 4), ("event", 0, 10), ("mix", 0), ("event", 0, 11)]
        beside = {(0, 0): [("tq", 4)], (0, 1): [12, ("outputs", 1), 13], (0, 2): [14, ("mix", 1)], (0, 3): [15],
                  (1, 0): [16, ("outputs", 2)], (1, 1): [17], (1, 2): [("mix", 2), 18], (1, 3): [19, 20, ("outputs", 3)],
                  (2, 0): [("mix", 3)]}
    else:
        events = {}
        for q in range(QUADS):
            for e in range(C_EVENTS):
                p = 4 * (9 * q + 7) + (e if e < C_LEAD + 2 else 9 + (e - C_LEAD - 2) * 27 // (C_EVENTS - C_LEAD - 2))
                events.setdefault(p, []).append(("event", q, e))
            events.setdefault(4 * (9 * q + 7) + 33, []).append(("outputs", q))
            events.setdefault(4 * (9 * q + 8) + 33, []).append(("mix", q))
        for b in range(2, blocks):
            for m in range(4):
                out += pieces(b, (m,))
                if m == 0:
                    out.append(("block", b - 1))
                if m == 1:
                    out.append(("split", b + LEAD))
                    if b in (3, 4, 5):
                        out.append(("mask", b - 3))
                if (b, m) == (2, 0):
                    out.append(("tq", 0))
                if m == 2 and is_rotated(layer, b - 1):
                    out.append(("tq", b - 1))
                out += events.get(4 * b + m, [])
        beside = {}
        for e in range(C_LEAD + 2, C_EVENTS):
            p = (e - C_LEAD - 2) * 8 // (C_EVENTS - C_LEAD - 2)
            beside.setdefault(divmod(p, 4), []).append(e)
        beside[0, 0] = [("block", blocks - 1)] + beside[0, 0]
        beside[1, 3].append(("outputs", 3))
        beside[2, 0] = [("mix", 3)]
    for q, m in [(q, m) for q in (0, 1) for m in range(4)] + [(2, 0), (2, 1), (3, 0), (3, 1), (2, 2), (2, 3), (3, 2), (3, 3)]:
        if (q, m) == (3, 3):
            out.append(("turn_next", 0))
        out.append(("opiece", q, m))
        if (q, m) == (3, 1):
            out += [("split_lo", blocks + 2 + LEAD), ("scale", 0)]
        out += [x if isinstance(x, tuple) else ("event", 0 if layer % 3 == 0 else 3, x) for x in beside.get((q, m), [])]
        if (q, m) in ((0, 2), (1, 0)):
            out.append(("split", blocks + q + LEAD))
        if (q, m) == (2, 1):
            out.append(("split_hi", blocks + 2 + LEAD))
    return out


def block_bank(b):
    return 2 if b == 2 else b % 2


def bank_before(b):
    return None if b <= 2 else 0 if b == 4 else b - 2


A_LEAD, C_LEAD = 3, 5
C_EVENTS = C_LEAD + QUAD * C_GROUPS + 2


def event_units(layer, q, e):
    lead, n, first = (A_LEAD, A_HEADS, 0) if layer % 3 == 0 else (C_LEAD, QUAD * C_GROUPS, QUAD * C_GROUPS * q)
    scores, turn, values = e, e - lead, e - lead - 2
    return [first + u if 0 <= u < n else None for u in (scores, turn, values)]


def mamba_order():
    units = 2 * GROUPS
    z = [(nb, k, t) for nb in range(1, 4) for k in range(2) for t in range(NT)]
    outs = [(k, t, nb) for k in range(4) for t in range(NT) for nb in range(2)]

    def piece(n, half):
        if n < len(z):
            nb, k, t = z[n]
            step = [("z", nb, k, t, half)]
            if (t, half) == (0, 1):
                step.append(("split", 2 * (nb - 1) + k + LEAD))
            if (k, t, half) == (1, 1, 1):
                step.append(("zout", nb))
            return step
        k, t, nb = outs[n - len(z)]
        step = [("out", k, t, nb, half)]
        if half and t == nb and (k, t) != (3, 1):
            step.append(("split", 6 + 2 * k + nb + LEAD))
        return step

    out = []
    lead = 6
    splits = []
    for n in range(lead):
        for half in range(2):
            if (n, half) == (lead - 1, 1):
                out += [("cs",), ("first", 0)]
            x = 2 * (2 * (n - lead + 3) + half)
            for step in piece(n, half):
                (splits if step[0] == "split" else out).append(step)
            if 0 <= x < 8:
                out += [("x", x), ("x", x + 1)]
            if x in (2, 6):
                out.append(splits.pop(0))
    out += splits
    for s in range(len(z) + len(outs) - lead):
        if s + 1 < units:
            out.append(("first", s + 1))
        if s % 2 == 0 and 0 <= s // 2 - 2 < GROUPS:
            out.append(("turn", s // 2 - 2))
        out += piece(lead + s, 0)
        if s < units:
            out.append(("second", s))
        if 0 < s <= units:
            out.append(("square", s - 1))
        if s % 2 and 0 <= (s - 3) // 2 < GROUPS:
            out.append(("scale", (s - 3) // 2))
        out += piece(lead + s, 1)
    return out


XS = 17408
NW = XS + NT * D
ARENA = 20480
COLS = 14336
M_R, M_SQ = 0, 2048
AT_P, AT_S = 0, 512
AT_ROT = 1024
AT_PT = 2048
AT_MASK = AT_PT + 3 * 384
AT_SM = AT_MASK + 3 * 384
AT_QKV = AT_SM + 3 * 1152
A_QT = AT_QKV
A_KT = A_QT + 2048
A_V = A_KT + 512
A_BIAS = A_V + 256
A_BO = A_BIAS + A_QKV
A_TMP = A_BO + D
assert A_TMP + 512 <= COLS
C_QT = AT_QKV
C_KT = C_QT + 2 * 1536
C_V = C_KT + 2 * 1536
assert C_V + 2 * 1536 <= XS
C_DIST = XS
R_FREQ = COLS + 4 * P
R_ARG = R_FREQ + 7 * HALF
GW_ROWS = R_ARG + 2 * NT * HALF
assert GW_ROWS + P <= XS
B_Z = 0
B_XC = 4096
B_G = B_XC
B_BT = B_XC + CT_X * SEQ
B_CT = B_BT + GROUPS * SEQ
B_XTOK = 12288
B_RL = 16384
B_ACC = B_RL
B_PADS = [B_Z + 512, B_Z + 1032, B_Z + INNER + 512, B_Z + INNER + 1032]
B_E = B_RL + 512
B_XDEC = B_E + 1024
B_ST = B_XDEC + 512
B_XD = B_ST + 512
B_TMP = B_XD + 512
B_BTOK = B_TMP + 256
B_CBM = B_BTOK + 128
B_JUNK = B_CBM + 256
assert B_JUNK + 256 <= ARENA


def trunk(nc, x, positions, norm_mix_w, norm_mlp_w, a_w_qkv, a_b_qkv, a_sinks, a_w_o, a_b_o,
          b_in_w, b_conv_w, b_conv_b, b_dt_bias, b_a_log, b_d, b_norm_w, b_out_w,
          c_w_qkv, c_w_o, mlp_w_up, mlp_w_down, final_norm_w, rope_freq, out):
    ctx = ExitStack()
    with ctx:
        def sb(name, shape, dt=F32):
            return ctx.enter_context(nc.sbuf_tensor(name, shape, dt))

        def sem(name):
            return ctx.enter_context(nc.semaphore(name))

        raw = sb("raw", [P, RAW, CHUNK])
        w_hi = sb("w_hi", [P, RING, CHUNK], F32R)
        w_lo = sb("w_lo", [P, RING, CHUNK], F32R)
        xt = sb("xt", [P, 2, 2 * KT, SEQ], F32R)
        h = sb("h", [P, NT, D])
        ar = sb("arena", [P, ARENA])
        ident = sb("ident", [P, P])
        tril = sb("tril", [P, P])
        strict = sb("strict", [P, P])
        ones = sb("ones", [P, P])
        zero16 = sb("zero16", [P, P], BF16)
        cosr = sb("cosr", [P, NT, HD])
        sinr = sb("sinr", [P, NT, HD])
        pos_f = sb("pos_f", [P, NT])
        ssq = sb("ssq", [P, NT])
        var = sb("var", [P, NT])
        rstd = sb("rstd", [P, NT])
        mhalf = sb("mhalf", [P, 16])
        sinks = sb("sinks", [P, A_HEADS])
        nsinks = sb("nsinks", [P, A_HEADS])
        negmax = sb("negmax", [P, C_GROUPS, NT, A_HEADS])
        den = sb("den", [P, NT, A_HEADS])
        rden = sb("rden", [P, NT, A_HEADS])
        esk = sb("esk", [P, NT, A_HEADS])
        convw = sb("convw", [P, TAPS, CT_ALL])
        convb = sb("convb", [P, CT_ALL])
        gnw = sb("gnw", [P, CT_X])
        dtb = sb("dtb", [P, SSM_HEADS])
        alog = sb("alog", [P, SSM_HEADS])
        dskip = sb("dskip", [P, SSM_HEADS])
        dt = sb("dt", [P, NT, SSM_HEADS])
        dt_t = sb("dt_t", [P, NT, SSM_HEADS])
        dt_u = sb("dt_u", [P, NT, SSM_HEADS])
        da = sb("da", [P, NT, SSM_HEADS])
        decay = sb("decay", [P, SSM_HEADS])
        ecs = sb("ecs", [P, SSM_HEADS])
        gss = sb("gss", [P, NT, GROUPS])
        grs = sb("grs", [P, NT, GROUPS])
        bank = [ctx.enter_context(nc.psum_tensor(f"bank{n}", [P, 512], F32)) for n in range(8)]

        def v(off, *dims):
            n = int(np.prod(dims))
            a = ar[:, off:off + n]
            if len(dims) == 1:
                return a
            names = "abcd"[:len(dims)]
            return a.rearrange(f"p ({' '.join(names)}) -> p {' '.join(names)}",
                               **{k: d for k, d in zip(names[1:], dims[1:])})

        xs = v(XS, NT, D)
        convw_rows, convb_rows = v(COLS, P), v(COLS + P, P)[0:CT_ALL, :]
        gnw_rows = v(GW_ROWS, P)[0:CT_X, :]
        pos_rows, pos_rows_f = v(COLS + 2 * P, P)[0:NT, :].bitcast(I32), v(COLS + 3 * P, P)[0:NT, :]
        nw = v(NW, D)

        raw_in = [sem(f"raw_in{n}") for n in range(RAW)]
        hi_done, lo_done, chunk_done = sem("hi_done"), sem("lo_done"), sem("chunk_done")
        first_hi, first_lo = sem("first_hi"), sem("first_lo")
        in_h = [sem(f"in_h{t}") for t in range(NT)]
        in_pos, in_first, in_small, in_nw0, in_nw, in_bias, in_sink = (sem(n) for n in ("in_pos", "in_first", "in_small", "in_nw0", "in_nw", "in_bias", "in_sink"))
        pool_const, dist_made, cols_done, rope_arg, rope_tab, vec_const = (sem(n) for n in ("pool_const", "dist_made", "cols_done", "rope_arg", "rope_tab", "vec_const"))
        ssq_done, rstd_done, var_done, xs_done = sem("ssq_done"), sem("rstd_done"), sem("var_done"), sem("xs_done")
        t_done, xhi_done, xlo_done = sem("t_done"), sem("xhi_done"), sem("xlo_done")
        h_done = sem("h_done")
        relu_done, sq_done, sqt_done, uhi_done, ulo_done = sem("relu_done"), sem("sq_done"), sem("sqt_done"), sem("uhi_done"), sem("ulo_done")
        biased, rope_mul, roped, qt_done, qt_out, v_out, bo_added, wo_done, tile_done = (sem(n) for n in ("biased", "rope_mul", "roped", "qt_done", "qt_out", "v_out", "bo_added", "wo_done", "tile_done"))
        sc_done, sm_done, pr_done, pt_done, pt_out, pv_done = (sem(n) for n in ("sc_done", "sm_done", "pr_done", "pt_done", "pt_out", "pv_done"))
        esk_arg, esk_done, o_out = sem("esk_arg"), sem("esk_done"), sem("o_out")
        pad_done, conv_step, conv_out = (sem(n) for n in ("pad_done", "conv_step", "conv_out"))
        dt_pre, dt_e, dt_ln, dt_done, cs_done, cs_dec, cs_exp, dec_done = (sem(n) for n in ("dt_pre", "dt_e", "dt_ln", "dt_done", "cs_done", "cs_dec", "cs_exp", "dec_done"))
        xt_done, xtok_out_a, xtok_out_v, z_out = sem("xt_done"), sem("xtok_out_a"), sem("xtok_out_v"), sem("z_out")
        rl_done, xd_done, xdec_done, cb_done, cbm_done, seg_done, e_done, m_done = (sem(n) for n in ("rl_done", "xd_done", "xdec_done", "cb_done", "cbm_done", "seg_done", "e_done", "m_done"))
        btok_out, st_done, st_out, y_done, y_out, y_whole, gate_done, gss_done, grs_done, gvar_done, ycomb, gn_done = (sem(n) for n in ("btok_out", "st_done", "st_out", "y_done", "y_out", "y_whole", "gate_done", "gss_done", "grs_done", "gvar_done", "ycomb", "gn_done"))
        out_done, chain = sem("out_done"), sem("chain")

        block = ctx.enter_context(nc.Block())

        def k_view(w):
            return w.rearrange("(k p) n -> p k n", p=P)

        def relus(step0, j):
            return ([], [0, 1], [], [2], [3])[j] if step0 == 0 and j < 5 else [j - 1] if 0 < j < 5 else []

        def z_chunk(l, nb, k):
            return FIRST[l, "z0"] + k if nb == 0 else FIRST[l, "z"] + 2 * (nb - 1) + k

        def mix_slot(k):
            return (k + KT) % (2 * KT)

        def obank(l, n):
            return (n + (A_BLOCKS if l % 3 == 0 else 9 * QUADS)) % 2

        def of(n, i, per):
            return n if i is None else i * per + n

        @block.sync
        def _(sp):
            def row(w, n):
                return w.rearrange("(a n) -> a n", a=1).to_broadcast([P, n])

            sp.dma_start(h[:, 0, :], x[0, 0:P, :]).then_inc(in_h[0], 16)
            sp.dma_start(pos_rows, positions[0].rearrange("(t p) -> t p", p=P)).then_inc(in_pos, 16)
            sp.dma_start(v(R_FREQ, HALF), row(rope_freq, HALF)).then_inc(in_pos, 16)
            w = k_view(a_w_qkv[0])[:, :, A_ORDER[0][1]:A_ORDER[0][1] + QW]
            first = raw[:, 0, :].rearrange("p (k n) -> p k n", k=KT)
            sp.dma_start(first[:, 0:4, :], w[:, 0:4, :]).then_inc(in_first, 16)
            sp.dma_start(nw, row(norm_mix_w[0], D)).then_inc(in_nw0, 16)
            sp.dma_start(first[:, 4:KT, :], w[:, 4:KT, :]).then_inc(raw_in[0], 16)
            sp.dma_start(h[:, 1, :], x[0, P:SEQ, :]).then_inc(in_h[1], 16)

            def load(c, src, kts, i=None, per=0):
                if c >= RAW:
                    sp.wait_ge(lo_done, of(c - RAW + 1, i, per))
                n = kts * src.shape[-1]
                dst = raw[:, c % RAW, 0:n].rearrange("p (k n) -> p k n", k=kts)
                sp.dma_start(dst, src).then_inc(raw_in[c % RAW], 16)

            def mlp(l, i=None, step0=0):
                wu, wd = k_view(mlp_w_up[l]), k_view(mlp_w_down[l])
                c = FIRST[l, "mlp"] + step0 * MLP_PER
                for j in range(4):
                    at = of((step0 * 4 + j) * 256, i, 1024)
                    load(c + j, wu[:, :, bass.ds(at, 256)], KT, i, MLP_PER)
                for j in range(4):
                    at = of(step0 * 8 + j // 2 * 4, i, 8)
                    load(c + 4 + j, wd[:, bass.ds(at, 4), (j % 2) * 512:(j % 2 + 1) * 512], 4, i, MLP_PER)

            def o_chunks(l, w):
                for q in range(QUADS):
                    load(FIRST[l, "o"] + q, w[:, 2 * q:2 * q + 2, :], 2)

            for l in range(DEPTH):
                if l % 3 == 0:
                    w = k_view(a_w_qkv[l // 3])
                    for n, (_, col) in enumerate(A_ORDER):
                        if (l, n) == (0, 0):
                            continue
                        load(FIRST[l, "qkv"] + n, w[:, :, col:col + QW], KT)
                    o_chunks(l, k_view(a_w_o[l // 3]))
                elif l % 3 == 1:
                    w = k_view(b_in_w[0])

                    def z_load(nb):
                        for k in range(2):
                            load(z_chunk(l, nb, k), w[:, 4 * k:4 * k + 4, nb * 512:(nb + 1) * 512], 4)

                    z_load(0)
                    load(FIRST[l, "dt"], w[:, :, INNER + CONV:INNER + CONV + SSM_HEADS], KT)
                    with sp.Fori(0, 4) as i:
                        for j in range(4):
                            load(FIRST[l, "xbc"] + j, w[:, :, bass.ds(i * 1024 + (INNER + j * 256), 256)], KT, i, 4)
                    for nb in range(1, 4):
                        z_load(nb)
                    w = k_view(b_out_w[0])
                    for k in range(4):
                        for nb in range(2):
                            load(FIRST[l, "out"] + 2 * k + nb, w[:, 4 * k:4 * k + 4, nb * 512:(nb + 1) * 512], 4)
                else:
                    w = k_view(c_w_qkv[0])
                    for q in range(QUADS):
                        for j, (kind, g) in enumerate(C_ORDER):
                            col = "qkv".index(kind) * C_GROUPS * D + g * D + q * QW
                            load(FIRST[l, "qkv"] + 9 * q + j, w[:, :, col:col + QW], KT)
                    o_chunks(l, k_view(c_w_o[0]))
                mlp(l)
                with sp.Fori(0, MLP_STEPS - 1) as i:
                    mlp(l, i, 1)
            for t in range(NT):
                sp.wait_ge(xs_done, NT * NORMS["final"] + t + 1)
                sp.dma_start(out[0, t * P:(t + 1) * P, :], xs[:, t, :]).then_inc(out_done, 16)
            sp.wait_ge(out_done, 16 * NT)

        @block.gpsimd
        def _(pool):
            chained = [0]

            def link(ins):
                chained[0] += 1
                ins.then_inc(pool_const, 1)
                pool.wait_ge(pool_const, chained[0])

            def row(w, n):
                return w.rearrange("(a n) -> a n", a=1).to_broadcast([P, n])

            link(pool.memset(ident[:, :], 0.0))
            link(pool.affine_select(out=ident[:, :], in_=ident[:, :], compare_op=ALU.not_equal, fill=1.0,
                                    base=0, pattern=[[-1, P]], channel_multiplier=1))
            pool.memset(tril[:, :], 1.0)
            pool.memset(ones[:, :], 1.0)
            pool.memset(mhalf[:, :], -0.5)
            link(pool.memset(strict[:, :], 1.0))
            pool.affine_select(out=tril[:, :], in_=tril[:, :], compare_op=ALU.is_ge, fill=0.0,
                               base=0, pattern=[[1, P]], channel_multiplier=-1)
            link(pool.affine_select(out=strict[:, :], in_=strict[:, :], compare_op=ALU.is_ge, fill=0.0,
                                    base=-1, pattern=[[-1, P]], channel_multiplier=1))

            def distances(dst):
                pool.iota(dst[:, 0:P], pattern=[[-1, P]], base=0, channel_multiplier=1)
                pool.iota(dst[:, P:3 * P], pattern=[[-1, 2 * P]], base=P, channel_multiplier=1).then_inc(dist_made, 1)

            def load_nw(w):
                pool.dma_start(nw, row(w, D)).then_inc(in_nw, 16)

            def rstds(name, tiles=range(NT)):
                n = NT * NORMS[name]
                for t in tiles:
                    pool.wait_ge(ssq_done, n + t + 1)
                    pool.tensor_scalar(var[:, t:t + 1], ssq[:, t:t + 1], 1.0 / D, EPS, ALU.mult, ALU.add).then_inc(var_done, 1)
                    pool.wait_ge(var_done, n + t + 1)
                    pool.tensor_tensor(rstd[:, t:t + 1], var[:, t:t + 1], mhalf[:, 0:1], ALU.pow).then_inc(rstd_done, 1)

            rstds((0, "norm"), [0])
            pool.dma_start(convb_rows, b_conv_b[0].rearrange("(c p) -> c p", p=P)).then_inc(in_small, 16)
            pool.dma_start(convw_rows, b_conv_w[0].rearrange("k (c p) -> (k c) p", p=P)).then_inc(in_small, 16)
            pool.dma_start(gnw_rows, b_norm_w[0].rearrange("(c p) -> c p", p=P)).then_inc(in_small, 16)
            pool.dma_start(dtb[:, :], row(b_dt_bias[0], SSM_HEADS)).then_inc(in_small, 16)
            pool.dma_start(alog[:, :], row(b_a_log[0], SSM_HEADS)).then_inc(in_small, 16)
            pool.dma_start(dskip[:, :], row(b_d[0], SSM_HEADS)).then_inc(in_small, 16)
            rstds((0, "norm"), [1])
            for l in range(DEPTH):
                if l:
                    rstds((l, "norm"))
                if l % 3 == 0:
                    a = l // 3
                    if l:
                        pool.wait_ge(h_done, H_END[l - 1, "mlp"])
                    pool.dma_start(v(A_BIAS, A_QKV), row(a_b_qkv[a], A_QKV)).then_inc(in_bias, 16)
                    pool.dma_start(v(A_BO, D), row(a_b_o[a], D)).then_inc(in_sink, 16)
                    if l:
                        pool.wait_ge(o_out, QUADS)
                    pool.dma_start(sinks[:, :], row(a_sinks[a], A_HEADS)).then_inc(in_sink, 16)

                if l % 3 != 1:
                    pool.wait_ge(t_done, T_FIRST[l, "norm"] + KT // 2)
                    distances(v(C_DIST, 3 * P).bitcast(I32))

                def rotate_sum(b, width, dup=False):
                    n = ROPE_NO[l, b]
                    dst = v(AT_ROT + (n % 2) * 512, NT, 256)
                    p_, s_ = v(AT_P, NT, 256), v(AT_S, NT, 256)
                    for t in range(NT):
                        pool.wait_ge(rope_mul, NT * n + t + 1)
                        if t == 0 and n >= 2:
                            pool.wait_ge(qt_done, n - 1)
                        if dup:
                            for e in range(2):
                                o = dst[:, t, :].rearrange("p (g e d) -> p g e d", e=2, d=HD)[:, :, e, :]
                                ins = pool.tensor_tensor(o, p_[:, t, 0:width].rearrange("p (g d) -> p g d", d=HD),
                                                         s_[:, t, 0:width].rearrange("p (g d) -> p g d", d=HD), ALU.add)
                        else:
                            ins = pool.tensor_tensor(dst[:, t, :], p_[:, t, :], s_[:, t, :], ALU.add)
                        ins.then_inc(roped, 1)

                if l % 3 == 0:
                    for b in range(A_BLOCKS):
                        rotate_sum(b, A_KV * HD if b == 0 else QW, dup=b == 0)
                    pool.wait_ge(xs_done, NT * (NORMS[l, "norm"] + 1))
                    pool.wait_ge(in_sink, 32 * (a + 1))
                    for t in range(NT):
                        pool.tensor_tensor(h[:, t, :], h[:, t, :], v(A_BO, D), ALU.add).then_inc(bo_added, 1)
                elif l % 3 == 1:
                    pool.wait_ge(h_done, H_END[l - 1, "mlp"])
                    for n in range(4):
                        pool.memset(v(B_PADS[n], 2, 260)[:, :, 0:3], 0.0).then_inc(pad_done, 1)
                    pool.memset(v(B_ACC, 1), 0.0).then_inc(conv_out, 1)
                    xtok = v(B_XTOK, NT, INNER)

                    def by_head(col, g, n):
                        return col[:, HPG * g:HPG * g + HPG].unsqueeze(2).to_broadcast([P, HPG, n])

                    def segments(u):
                        g, c = u // 2, u % 2
                        if u:
                            pool.wait_ge(seg_done, u)
                        pool.tensor_tensor(v(B_RL, HPG, P), by_head(da[:, c, :], g, P),
                                           tril[:, :].unsqueeze(1).to_broadcast([P, HPG, P]), ALU.mult).then_inc(rl_done, 1)

                    def by_columns(u):
                        g, c = u // 2, u % 2
                        if u >= 2:
                            pool.wait_ge(y_out, u - 1)
                        xg = xtok[:, c, g * GW:(g + 1) * GW].rearrange("p (h d) -> p h d", d=HD)
                        pool.tensor_tensor(v(B_XD + c * 256, HPG, HD), xg, by_head(dskip, g, HD), ALU.mult).then_inc(xd_done, 1)
                        if c == 0:
                            if g >= 2:
                                pool.wait_ge(y_done, 2 * (g - 2) + 1)
                            pool.tensor_tensor(v(B_XDEC + (g % 2) * 256, HPG, HD), xg, by_head(decay, g, HD), ALU.mult).then_inc(xdec_done, 1)

                    def gate(u):
                        g, c = u // 2, u % 2
                        y = v(B_G, NT, INNER)[:, c, g * GW:(g + 1) * GW]
                        pool.wait_ge(z_out, 2 * (g // 2) + c + 1)
                        if c == 0:
                            pool.wait_ge(y_out, u + 1)
                        else:
                            pool.wait_ge(y_whole, g + 1)
                        pool.tensor_tensor(y, y, v(B_Z, NT, INNER)[:, c, g * GW:(g + 1) * GW], ALU.mult).then_inc(gate_done, 1)

                    def group_rstd(g):
                        pool.wait_ge(gss_done, 2 * g + 2)
                        pool.tensor_scalar(gss[:, :, g:g + 1], gss[:, :, g:g + 1], 1.0 / GW, EPS, ALU.mult, ALU.add).then_inc(gvar_done, 1)
                        pool.wait_ge(gvar_done, g + 1)
                        pool.tensor_tensor(grs[:, :, g:g + 1], gss[:, :, g:g + 1], mhalf[:, 0:2].unsqueeze(2), ALU.pow).then_inc(grs_done, 1)

                    pool.wait_ge(dt_done, 2)
                    pool.wait_ge(conv_out, 17)
                    segments(0)
                    pool.wait_ge(xtok_out_a, 4)
                    pool.wait_ge(xtok_out_v, 4)
                    pool.wait_ge(dec_done, 1)
                    by_columns(0)
                    for u in range(2 * GROUPS):
                        g, c = u // 2, u % 2
                        if u + 1 < 2 * GROUPS:
                            segments(u + 1)
                            by_columns(u + 1)
                        if u:
                            gate(u - 1)
                        if c and g:
                            group_rstd(g - 1)
                    gate(2 * GROUPS - 1)
                    group_rstd(GROUPS - 1)
                else:
                    for b in range(9 * QUADS):
                        if is_rotated(l, b):
                            rotate_sum(b, QW)
                pool.wait_ge(xs_done, NT * (NORMS[l, "norm"] + 1))
                load_nw(norm_mlp_w[l])
                rstds((l, "mlp"))
                pool.wait_ge(xs_done, NT * (NORMS[l, "mlp"] + 1))
                load_nw(norm_mix_w[l + 1] if l + 1 < DEPTH else final_norm_w)
            rstds("final")

        @block.scalar
        def _(act):
            def split(c, i=None, per=0, width=CHUNK):
                if c >= N_CHUNKS:
                    return
                if c == FIRST[1, "dt"]:
                    width = KT * SSM_HEADS
                use, per_use = c // RAW + 1, per // RAW
                act.wait_ge(raw_in[c % RAW], of(16 * use, i, 16 * per_use))
                if c >= RING:
                    act.wait_ge(chunk_done, of(c - RING + 1, i, per))
                act.activation(w_hi[:, c % RING, 0:width], raw[:, c % RAW, 0:width], ACT.Copy).then_inc(hi_done, 1)

            def square(end, t):
                if end:
                    act.wait_ge(h_done, end - 2 * (NT - 1 - t))
                else:
                    act.wait_ge(in_h[t], 16)
                act.activation(xs[:, t, :], h[:, t, :], ACT.Square, accum_out=ssq[:, t:t + 1]).then_inc(ssq_done, 1)

            def t_hi_norm(name, t):
                for n in (2 * t, 2 * t + 1):
                    k = n % 2 * 4
                    act.wait_ge(t_done, T_FIRST[name] + n + 1)
                    act.activation(xt[:, 0, k:k + 4, t * P:(t + 1) * P], bank[4 + n][:, :].rearrange("p (k n) -> p k n", k=4), ACT.Copy)\
                       .then_inc(xhi_done, 1)

            def norm(name, end, c):
                for t in range(NT):
                    square(end, t)
                    if t == 0:
                        split(c)
                    t_hi_norm(name, t)

            def t_hi(name, j, k, b):
                act.wait_ge(t_done, T_FIRST[name] + j + 1)
                act.activation(xt[:, 0, k:k + 2, :], bank[b][:, :].rearrange("p (k n) -> p k n", k=2), ACT.Copy).then_inc(xhi_done, 1)

            def mlp(l, i=None, step0=0):
                c, u = FIRST[l, "mlp"] + step0 * MLP_PER, 16 * l + 4 * step0
                for j in range(MLP_PER - (step0 == MLP_STEPS - 1)):
                    for k in relus(step0, j):
                        act.wait_ge(chunk_done, of(c + k + 1, i, MLP_PER))
                        act.activation(v(M_R, 4, 512)[:, k, :], bank[4 + k][:, :], ACT.Relu).then_inc(relu_done, 1)
                    split(c + j + LEAD, i, MLP_PER)
                    if j in (1, 2, 3, 4):
                        k = j - 1
                        if step0 == 0 and k < 2:
                            act.wait_ge(sqt_done, 2 * l + k + 1)
                            src = bank[4 + k][:, :].rearrange("p (k n) -> p k n", k=2)
                        else:
                            act.wait_ge(sq_done, of(u + k + 1, i, 4))
                            src = v(M_SQ, 4, 2, SEQ)[:, k]
                        act.activation(xt[:, 0, KT + 2 * k:KT + 2 * k + 2, :], src, ACT.Copy).then_inc(uhi_done, 1)

            def attention(l):
                ng = 1 if l % 3 == 0 else C_GROUPS
                u0, h0, w = UNIT0[l], HEAD0[l], 3 * P * ng
                slots = 4 if ng == 1 else 3
                sm = v(AT_SM, slots, w)
                c = FIRST[l, "qkv"]

                def exps(n):
                    act.wait_ge(sm_done, 2 * (u0 + (n + 1) * ng))
                    for b in range(NT):
                        at = slice(0, P * ng) if b == 0 else slice(P * ng, w)
                        act.activation(sm[:, n % slots, at], sm[:, n % slots, at], ACT.Exp, scale=-1.0,
                                       bias=negmax[:, ng - 1, b, n:n + 1], accum_out=den[:, b, n:n + 1]).then_inc(pr_done, 1)

                for step in order(l):
                    what, q, m = step[0], step[1], step[-1]
                    if what in ("split", "split_hi"):
                        split(c + q)
                    elif what == "block" and not is_rotated(l, q):
                        act.wait_ge(chunk_done, c + q + 1)
                        vv = v(C_V + q // 9 % 2 * 1536, NT, C_GROUPS, QW)[:, :, C_ORDER[q % 9][1], :]
                        act.activation(vv, bank[block_bank(q)][:, :].rearrange("p (t n) -> p t n", t=NT), ACT.Copy).then_inc(v_out, 1)
                    elif what == "tq":
                        n = ROPE_NO[l, q]
                        act.wait_ge(qt_done, n + 1)
                        if l % 3 == 0:
                            dst = v(A_KT, 2, SEQ) if q == 0 else v(A_QT, 4, 2, SEQ)[:, q - 1]
                        else:
                            kind, g = C_ORDER[q % 9]
                            dst = v((C_QT if kind == "q" else C_KT) + q // 9 % 2 * 1536, C_GROUPS, 2, SEQ)[:, g]
                        act.activation(dst, bank[7][:, :].rearrange("p (k n) -> p k n", k=2), ACT.Copy).then_inc(qt_out, 1)
                    elif what == "mix":
                        t_hi((l, "mix"), q, KT + 2 * q, 7)
                    elif what == "event":
                        _, turn, _ = event_units(l, q, m)
                        if m == (1 if ng == 1 else 3):
                            exps(QUAD * q)
                        if turn is not None:
                            act.wait_ge(pt_done, u0 + turn + 1)
                            if turn >= 3:
                                act.wait_ge(pv_done, u0 + turn - 2)
                            act.activation(v(AT_PT + turn % 3 * 384, 384), bank[6][:, 0:3 * P], ACT.Copy).then_inc(pt_out, 1)
                            n = turn // ng
                            if ng == 1 and n % QUAD == QUAD - 1:
                                e = slice(n - QUAD + 1, n + 1)
                                act.wait_ge(esk_arg, QUADS * (l // 3) + n // QUAD + 1)
                                act.activation(esk[:, :, e], esk[:, :, e], ACT.Exp).then_inc(esk_done, 1)
                            if turn % ng == 0 and (n + 1 < A_HEADS if ng == 1 else n % QUAD < QUAD - 1):
                                exps(n + 1)

            square(0, 0)
            act.wait_ge(in_first, 16)
            act.activation(w_hi[:, 0, 0:CHUNK // 2], raw[:, 0, 0:CHUNK // 2], ACT.Copy).then_inc(first_hi, 1)
            act.wait_ge(raw_in[0], 16)
            act.activation(w_hi[:, 0, CHUNK // 2:], raw[:, 0, CHUNK // 2:], ACT.Copy).then_inc(hi_done, 1)
            t_hi_norm((0, "norm"), 0)
            square(0, 1)
            split(1)
            act.wait_ge(rope_arg, 1)
            for e in range(2):
                act.activation(cosr[:, :, e * HALF:(e + 1) * HALF], v(R_ARG, 2, NT, HALF)[:, 0], ACT.Sin)
                act.activation(sinr[:, :, e * HALF:(e + 1) * HALF], v(R_ARG, 2, NT, HALF)[:, 1], ACT.Sin, scale=(-1.0, 1.0)[e])\
                   .then_inc(rope_tab, 1)
            split(2)
            t_hi_norm((0, "norm"), 1)
            for l in range(DEPTH):
                if l:
                    norm((l, "norm"), H_END[l - 1, "mlp"], FIRST[l - 1, "mlp"] + MLP_STEPS * MLP_PER - 1 + LEAD)
                if l % 3 != 1:
                    attention(l)
                elif l % 3 == 1:
                    c = FIRST[l, "xbc"]
                    z0, y_all = FIRST[l, "z0"], v(B_G, NT, INNER)

                    def z_out_of(nb):
                        act.wait_ge(chunk_done, z_chunk(l, nb, 1) + 1)
                        for t in range(NT):
                            act.activation(v(B_Z, NT, INNER)[:, t, nb * 512:(nb + 1) * 512],
                                           bank[2 * (nb % 2) + t][:, :], ACT.Silu).then_inc(z_out, 1)

                    split(z0 + LEAD)
                    split(z0 + 1 + LEAD)
                    z_out_of(0)
                    act.wait_ge(in_small, 16 * SMALL_LOADS)
                    act.activation(alog[:, :], alog[:, :], ACT.Exp).then_inc(dt_e, 1)
                    act.wait_ge(dt_pre, 2)
                    act.activation(dt_t[:, :, :], dt_t[:, :, :], ACT.Exp).then_inc(dt_e, 1)
                    act.wait_ge(dt_e, 2)
                    act.activation(dt_t[:, :, :], dt_t[:, :, :], ACT.Ln, bias=1.0).then_inc(dt_ln, 1)
                    split(z0 + 2 + LEAD)
                    act.wait_ge(pad_done, 4)
                    act.wait_ge(vec_const, 4)
                    with act.Fori(0, 4) as i:
                        act.wait_ge(conv_out, of(1, i, 4))
                        for j in range(4):
                            split(c + j + LEAD, i, 4)
                            act.wait_ge(chunk_done, of(c + j + 1, i, 4))
                            for e in range(2):
                                ct = i * 8 + (2 * j + e)
                                act.activation(v(B_ACC + j * 512, 2, 256)[:, e, :], bank[4 + j][:, e * SEQ:(e + 1) * SEQ], ACT.Identity,
                                               scale=convw[:, 3, bass.ds(ct, 1)], bias=convb[:, bass.ds(ct, 1)])
                            act.activation(v(B_PADS[j], 2, 260)[:, :, 3:259], bank[4 + j][:, :].rearrange("p (k n) -> p k n", k=2), ACT.Copy)\
                               .then_inc(pad_done, 1)
                            for k in ([j - 1] if j else []) + ([3] if j == 3 else []):
                                act.wait_ge(conv_step, of(6 * (k + 1), i, 24))
                                act.activation(ar[:, bass.ds(i * 2048 + (B_XC + k * 512), 512)], v(B_ACC + k * 512, 512), ACT.Silu)\
                                   .then_inc(conv_out, 1)
                    for what, *n in mamba_order():
                        if what == "split":
                            split(FIRST[l, "z"] + n[0])
                        elif what == "x" and n[0] % 2:
                            act.wait_ge(xt_done, n[0] + 1)
                            act.activation(v(B_XTOK, 8, 512)[:, n[0], :], bank[4 + n[0] % 4][:, :], ACT.Copy).then_inc(xtok_out_a, 1)
                        elif what == "cs":
                            act.wait_ge(cs_done, 1)
                            act.activation(ecs[:, :], bank[7][:, 0:SSM_HEADS], ACT.Exp).then_inc(cs_exp, 1)
                            act.wait_ge(cs_dec, 2)
                            act.activation(decay[:, :], decay[:, :], ACT.Exp).then_inc(cs_exp, 1)
                        elif what == "zout":
                            z_out_of(n[0])
                        elif what == "first":
                            u = n[0]
                            act.wait_ge(seg_done, u + 1)
                            if u >= 2:
                                act.wait_ge(y_done, u - 1)
                            act.activation(v(B_E + (u % 2) * 512, 512), bank[5][:, :], ACT.Exp).then_inc(e_done, 1)
                        elif what == "second" and n[0] % 2 == 0:
                            g = n[0] // 2
                            act.wait_ge(y_out, n[0] + 1)
                            if g >= 2:
                                act.wait_ge(y_done, 2 * (g - 2) + 2)
                            act.activation(v(B_ST + (g % 2) * 256, 256), bank[6][:, GW:2 * GW], ACT.Copy).then_inc(st_out, 1)
                        elif what == "square":
                            g, c = n[0] // 2, n[0] % 2
                            act.wait_ge(gate_done, n[0] + 1)
                            if n[0]:
                                act.wait_ge(gss_done, n[0])
                            act.activation(v(B_JUNK, 256), y_all[:, c, g * GW:(g + 1) * GW], ACT.Square,
                                           accum_out=gss[:, c, g:g + 1]).then_inc(gss_done, 1)
                        elif what == "scale":
                            g = n[0]
                            act.wait_ge(grs_done, g + 1)
                            for t in range(NT):
                                y = y_all[:, t, g * GW:(g + 1) * GW]
                                ins = act.activation(y, y, ACT.Identity, scale=grs[:, t, g:g + 1])
                            ins.then_inc(gn_done, 1)
                        elif what == "turn":
                            g = n[0]
                            act.wait_ge(t_done, T_FIRST[l, "mix"] + g + 1)
                            for k in range(2):
                                ins = act.activation(xt[:, 0, mix_slot(2 * g + k), :], bank[7][:, k * SEQ:(k + 1) * SEQ], ACT.Identity,
                                                     scale=gnw[:, 2 * g + k:2 * g + k + 1])
                            ins.then_inc(xhi_done, 1)
                norm((l, "mlp"), H_END[l, "mix"], FIRST[l, "mlp"] - 1 + LEAD)
                mlp(l)
                with act.Fori(0, MLP_STEPS - 2) as i:
                    mlp(l, i, 1)
                mlp(l, None, MLP_STEPS - 1)
            for t in range(NT):
                square(H_END[DEPTH - 1, "mlp"], t)

        @block.vector
        def _(dve):
            chained = [0]

            def link(ins):
                chained[0] += 1
                ins.then_inc(chain, 1)
                dve.wait_ge(chain, chained[0])

            def split(c, i=None, per=0, width=CHUNK):
                if c >= N_CHUNKS:
                    return
                if c == FIRST[1, "dt"]:
                    width = KT * SSM_HEADS
                dve.wait_ge(hi_done, of(c + 1, i, per))
                if c >= RING:
                    dve.wait_ge(chunk_done, of(c - RING + 1, i, per))
                dve.tensor_tensor(w_lo[:, c % RING, 0:width], raw[:, c % RAW, 0:width],
                                  w_hi[:, c % RING, 0:width].bitcast(F32), ALU.subtract).then_inc(lo_done, 1)

            def scale(name, t):
                n = NORMS[name]
                if n:
                    dve.wait_ge(in_nw, 16 * n)
                else:
                    dve.wait_ge(in_nw0, 16)
                dve.wait_ge(rstd_done, NT * n + t + 1)
                dve.scalar_tensor_tensor(out=xs[:, t, :], in0=h[:, t, :], scalar=rstd[:, t:t + 1], in1=nw,
                                         op0=ALU.mult, op1=ALU.mult).then_inc(xs_done, 1)

            def t_lo_norm(name, t):
                for n in (2 * t, 2 * t + 1):
                    k = n % 2 * 4
                    dve.wait_ge(xhi_done, T_FIRST[name] + n + 1)
                    dve.tensor_tensor(xt[:, 1, k:k + 4, t * P:(t + 1) * P], bank[4 + n][:, :].rearrange("p (k n) -> p k n", k=4),
                                      xt[:, 0, k:k + 4, t * P:(t + 1) * P].bitcast(F32), ALU.subtract).then_inc(xlo_done, 1)

            def t_lo(name, j, k, b):
                dve.wait_ge(xhi_done, T_FIRST[name] + j + 1)
                dve.tensor_tensor(xt[:, 1, k:k + 2, :], bank[b][:, :].rearrange("p (k n) -> p k n", k=2),
                                  xt[:, 0, k:k + 2, :].bitcast(F32), ALU.subtract).then_inc(xlo_done, 1)

            def add(dst, b):
                dve.tensor_tensor(dst, bank[b][:, :], dst, ALU.add).then_inc(h_done, 1)

            def residual(name, c_end, tile):
                dve.wait_ge(tile_done, tile)
                for nb in range(2):
                    add(h[:, 0, nb * 512:(nb + 1) * 512], 2 * nb)
                scale(name, 0)
                for nb in range(2):
                    dve.wait_ge(chunk_done, c_end - 1 + nb)
                    add(h[:, 1, nb * 512:(nb + 1) * 512], 2 * nb + 1)
                    if nb == 0 and name != "final":
                        t_lo_norm(name, 0)
                split(c_end - 1 + LEAD)
                scale(name, 1)
                if name != "final":
                    t_lo_norm(name, 1)

            def mlp(l, i=None, step0=0):
                c, u = FIRST[l, "mlp"] + step0 * MLP_PER, 16 * l + 4 * step0
                for j in range(MLP_PER - (step0 == MLP_STEPS - 1)):
                    for k in relus(step0, j):
                        dve.wait_ge(relu_done, of(u + k + 1, i, 4))
                        dve.tensor_tensor(v(M_SQ, 4, 512)[:, k, :], v(M_R, 4, 512)[:, k, :], v(M_R, 4, 512)[:, k, :], ALU.mult).then_inc(sq_done, 1)
                    split(c + j + LEAD, i, MLP_PER)
                    if j in (1, 2, 3, 4):
                        k = j - 1
                        dve.wait_ge(uhi_done, of(u + k + 1, i, 4))
                        src = bank[4 + k][:, :].rearrange("p (k n) -> p k n", k=2) if step0 == 0 and k < 2 else v(M_SQ, 4, 2, SEQ)[:, k]
                        dve.tensor_tensor(xt[:, 1, KT + 2 * k:KT + 2 * k + 2, :], src,
                                          xt[:, 0, KT + 2 * k:KT + 2 * k + 2, :].bitcast(F32), ALU.subtract).then_inc(ulo_done, 1)

            def masks(l, g, window, dilation):
                dist = v(C_DIST, 3 * P).bitcast(I32)
                f, m, r = v(C_DIST + 384, 3 * P), v(C_DIST + 768, 3 * P), v(C_DIST + 1152, 3 * P)
                o = v(AT_MASK, 3, 384)[:, g, :]
                if g == 0:
                    dve.wait_ge(dist_made, 1 + [0, 2, 3].index(l))
                    link(dve.tensor_copy(f, dist))
                link(dve.tensor_scalar(m, f, float(window), None, ALU.is_le))
                link(dve.scalar_tensor_tensor(out=o, in0=f, scalar=0.0, in1=m, op0=ALU.is_ge, op1=ALU.mult))
                if dilation > 1:
                    link(dve.tensor_scalar(r.bitcast(I32), dist, dilation - 1, None, ALU.bitwise_and))
                    link(dve.tensor_copy(m, r.bitcast(I32)))
                    link(dve.scalar_tensor_tensor(out=o, in0=m, scalar=0.0, in1=o, op0=ALU.is_equal, op1=ALU.mult))
                link(dve.tensor_scalar(o, o, -1.0, BIG, ALU.add, ALU.mult))

            def rotate(n, width, src):
                nh = width // HD
                for t in range(NT):
                    if n:
                        dve.wait_ge(roped, NT * (n - 1) + t + 1)
                    x_ = src(t).rearrange("p (h d) -> p h d", d=HD)
                    p_ = v(AT_P, NT, 256)[:, t, 0:width].rearrange("p (h d) -> p h d", d=HD)
                    s_ = v(AT_S, NT, 256)[:, t, 0:width].rearrange("p (h d) -> p h d", d=HD)
                    dve.tensor_tensor(p_, x_, cosr[:, t, :].unsqueeze(1).to_broadcast([P, nh, HD]), ALU.mult)
                    dve.tensor_tensor(s_[:, :, 0:HALF], x_[:, :, HALF:HD], sinr[:, t, 0:HALF].unsqueeze(1).to_broadcast([P, nh, HALF]), ALU.mult)
                    dve.tensor_tensor(s_[:, :, HALF:HD], x_[:, :, 0:HALF], sinr[:, t, HALF:HD].unsqueeze(1).to_broadcast([P, nh, HALF]), ALU.mult)\
                       .then_inc(rope_mul, 1)

            def attention(l):
                ng = 1 if l % 3 == 0 else C_GROUPS
                u0, h0, w = UNIT0[l], HEAD0[l], 3 * P * ng
                slots = 4 if ng == 1 else 3
                sm, mask = v(AT_SM, slots, w), v(AT_MASK, 3, 384)
                c, a = FIRST[l, "qkv"], l // 3
                bias, tmp, vv = v(A_BIAS, A_QKV), v(A_TMP, NT, QW), v(A_V, NT, P)

                def scores(u):
                    n, g = u // ng, u % ng
                    dve.wait_ge(sc_done, u0 + u + 1)
                    if g == 0 and n >= slots:
                        dve.wait_ge(pt_done, u0 + (n - slots + 1) * ng)
                    for b in range(NT):
                        k = P * (b + 1)
                        at = P * g if b == 0 else P * ng + 2 * P * g
                        src = slice(0, P) if b == 0 else slice(P, 3 * P)
                        if g:
                            dve.wait_ge(sm_done, 2 * (u0 + u) + b - 1)
                            first = negmax[:, g - 1, b, n:n + 1]
                        else:
                            first = nsinks[:, n:n + 1] if ng == 1 else 3e38
                        dve.tensor_tensor_reduce(out=sm[:, n % slots, at:at + k], in0=bank[4 + u % 2][:, src],
                                                 in1=mask[:, g, src], scale=-ATT_SCALE, scalar=first,
                                                 op0=ALU.add, op1=ALU.min,
                                                 accum_out=negmax[:, g, b, n:n + 1]).then_inc(sm_done, 1)
                    if ng == 1 and n % QUAD == QUAD - 1:
                        e = slice(n - QUAD + 1, n + 1)
                        dve.wait_ge(sm_done, 2 * (u0 + u + 1))
                        for b in range(NT):
                            ins = dve.tensor_tensor(esk[:, b, e], sinks[:, e], negmax[:, 0, b, e], ALU.add)
                        ins.then_inc(esk_arg, 1)

                def outputs(q):
                    e = slice(QUAD * q, QUAD * (q + 1))
                    dve.wait_ge(pr_done, 2 * (h0 + QUAD * (q + 1)))
                    src = den
                    if ng == 1:
                        dve.wait_ge(esk_done, QUADS * a + q + 1)
                        link(dve.tensor_tensor(rden[:, :, e], den[:, :, e], esk[:, :, e], ALU.add))
                        src = rden
                    link(dve.reciprocal(rden[:, :, e], src[:, :, e]))
                    dve.wait_ge(pv_done, u0 + QUAD * (q + 1) * ng)
                    for b in range(NT):
                        ins = dve.tensor_tensor(xs[:, b, q * QW:(q + 1) * QW].rearrange("p (h d) -> p h d", d=HD),
                                                bank[2 + q % 2][:, b * QW:(b + 1) * QW].rearrange("p (h d) -> p h d", d=HD),
                                                rden[:, b, e].unsqueeze(2).to_broadcast([P, QUAD, HD]), ALU.mult)
                    ins.then_inc(o_out, 1)

                for step in order(l):
                    what, q, m = step[0], step[1], step[-1]
                    if what in ("split", "split_lo"):
                        split(c + q)
                    elif what == "scale":
                        scale((l, "mlp"), 0)
                    elif what == "mask":
                        masks(l, q, *(C_PATTERNS[q] if ng > 1 else (A_WINDOW - 1, 1)))
                        if ng == 1:
                            dve.wait_ge(in_sink, 32 * (a + 1))
                            link(dve.tensor_scalar(nsinks[:, :], sinks[:, :], -1.0, None, ALU.mult))
                    elif what == "opiece":
                        if q == 2:
                            continue
                        n = 4 * min(q, 2) + m
                        if m < 3:
                            dve.wait_ge(wo_done, 9 * (QUAD0[l] // QUADS) + 3 * min(q, 2) + m + 1)
                        else:
                            dve.wait_ge(chunk_done, FIRST[l, "o"] + q + 1)
                        if n >= 4:
                            dve.wait_ge(h_done, H_END[l, "mix"] - O_ADDS + n - 3)
                        elif n == 0 and ng == 1:
                            dve.wait_ge(bo_added, NT * (a + 1))
                        add(h[:, m // 2, m % 2 * 512:(m % 2 + 1) * 512], obank(l, n))
                        if (q, m) == (3, 2):
                            t_lo_norm((l, "mlp"), 0)
                    elif what == "block" and is_rotated(l, q):
                        n = ROPE_NO[l, q]
                        dve.wait_ge(chunk_done, c + q + 1)
                        ps = bank[block_bank(q)][:, :].rearrange("p (t n) -> p t n", t=NT)
                        if ng > 1:
                            rotate(n, QW, lambda t: ps[:, t, :])
                            continue
                        k, width = A_ORDER[q][1], P if q == 0 else QW
                        if n:
                            dve.wait_ge(rope_mul, NT * n)
                        for t in range(NT):
                            if q == 0:
                                dve.tensor_tensor(vv[:, t, :], ps[:, t, P:QW], bias[:, k + P:k + QW], ALU.add)
                            dve.tensor_tensor(tmp[:, t, 0:width], ps[:, t, 0:width], bias[:, k:k + width], ALU.add).then_inc(biased, 1)
                        dve.wait_ge(biased, NT * (A_BLOCKS * a + q + 1))
                        if n == 0:
                            dve.wait_ge(rope_tab, 2)
                            conv_columns()
                        rotate(n, width, lambda t: tmp[:, t, 0:width])
                    elif what == "outputs":
                        outputs(q)
                    elif what == "mix":
                        t_lo((l, "mix"), q, KT + 2 * q, 7)
                    elif what == "event":
                        u, _, _ = event_units(l, q, m)
                        if u is not None:
                            scores(u)

            def conv_columns():
                dve.wait_ge(cols_done, 2)
                dve.tensor_copy(convw[:, :, :], bank[3][:, 0:P].rearrange("p (k c) -> p k c", k=TAPS)).then_inc(vec_const, 1)
                dve.tensor_copy(convb[:, :], bank[3][:, P:P + CT_ALL]).then_inc(vec_const, 1)
                dve.tensor_copy(gnw[:, :], bank[3][:, P + CT_ALL:P + CT_ALL + CT_X]).then_inc(vec_const, 1)

            def rotary_arguments():
                freq, ang = v(R_FREQ, HALF), v(R_FREQ + HALF, NT, HALF)
                kk, arg = v(R_FREQ + 3 * HALF, 2, NT * HALF), v(R_ARG, 2, NT * HALF)
                two_pi = [6.28125, 0.0019350051879882812, 3.0198689e-07]
                dve.wait_ge(cols_done, 1)
                link(dve.tensor_copy(pos_f[:, :], bank[3][:, 2 * P:2 * P + NT]))
                for t in range(NT):
                    ins = dve.tensor_scalar(ang[:, t, :], freq, pos_f[:, t:t + 1], None, ALU.mult)
                link(ins)
                angles = v(R_FREQ + HALF, NT * HALF)
                for e, turn in ((0, 0.25), (1, 0.0)):
                    ins = dve.tensor_scalar(kk[:, e, :], angles, 0.5 / np.pi, turn, ALU.mult, ALU.add)
                link(ins)
                link(dve.tensor_scalar(kk, kk, 12582912.0, 12582912.0, ALU.add, ALU.subtract))
                link(dve.scalar_tensor_tensor(out=arg, in0=kk, scalar=-two_pi[0], in1=angles.unsqueeze(1).to_broadcast([P, 2, NT * HALF]),
                                              op0=ALU.mult, op1=ALU.add))
                for part in two_pi[1:]:
                    link(dve.scalar_tensor_tensor(out=arg, in0=kk, scalar=-part, in1=arg, op0=ALU.mult, op1=ALU.add))
                link(dve.tensor_scalar(arg[:, 0, :], arg[:, 0, :], np.pi / 2, None, ALU.add))
                dve.tensor_scalar(arg, arg, 3.1415925, -3.1415925, ALU.min, ALU.max).then_inc(rope_arg, 1)

            link(dve.memset(zero16[:, :], 0.0))
            dve.wait_ge(in_pos, 32)
            dve.tensor_copy(pos_rows_f, pos_rows).then_inc(vec_const, 1)
            rotary_arguments()
            for half, made, done in ((slice(0, CHUNK // 2), first_hi, first_lo), (slice(CHUNK // 2, CHUNK), hi_done, lo_done)):
                dve.wait_ge(made, 1)
                dve.tensor_tensor(w_lo[:, 0, half], raw[:, 0, half], w_hi[:, 0, half].bitcast(F32), ALU.subtract).then_inc(done, 1)
                if made is first_hi:
                    scale((0, "norm"), 0)
            t_lo_norm((0, "norm"), 0)
            scale((0, "norm"), 1)
            split(1)
            split(2)
            t_lo_norm((0, "norm"), 1)
            for l in range(DEPTH):
                if l % 3 == 0:
                    dve.wait_ge(in_bias, 16 * (l // 3 + 1))
                    attention(l)
                elif l % 3 == 1:
                    z0, c = FIRST[l, "z0"], FIRST[l, "xbc"]
                    dve.wait_ge(in_small, 16 * SMALL_LOADS)
                    for k in range(2):
                        split(z0 + k + LEAD)
                    dve.wait_ge(chunk_done, FIRST[l, "dt"] + 1)
                    for t in range(NT):
                        link(dve.tensor_tensor(dt_u[:, t, :], bank[2 + t][:, 0:SSM_HEADS], dtb[:, :], ALU.add))
                        dve.scalar_tensor_tensor(out=dt_t[:, t, :], in0=dt_u[:, t, :], scalar=-1.0, in1=dt_u[:, t, :],
                                                 op0=ALU.mult, op1=ALU.min).then_inc(dt_pre, 1)
                    split(z0 + 2 + LEAD)
                    with dve.Fori(0, 4) as i:
                        for j in range(4):
                            split(c + j + LEAD, i, 4)
                            for n in range(6):
                                k, e = 2 - n // 2, n % 2
                                if n < 2:
                                    dve.wait_ge(pad_done, of(4 + j + 1, i, 4))
                                else:
                                    dve.wait_ge(conv_step, of(6 * j + n - 1, i, 24))
                                acc = v(B_ACC + j * 512, 2, 256)[:, e, :]
                                dve.scalar_tensor_tensor(out=acc, in0=v(B_PADS[j], 2, 260)[:, e, k:k + 256],
                                                         scalar=convw[:, k, bass.ds(i * 8 + (2 * j + e), 1)], in1=acc,
                                                         op0=ALU.mult, op1=ALU.add).then_inc(conv_step, 1)
                    dve.wait_ge(dt_ln, 1)
                    link(dve.scalar_tensor_tensor(out=dt[:, :, :], in0=dt_u[:, :, :], scalar=0.0, in1=dt_t[:, :, :],
                                                  op0=ALU.max, op1=ALU.add))
                    for t in range(NT):
                        dve.scalar_tensor_tensor(out=da[:, t, :], in0=dt[:, t, :], scalar=-1.0, in1=alog[:, :],
                                                 op0=ALU.mult, op1=ALU.mult).then_inc(dt_done, 1)
                    y_all = v(B_G, NT, INNER)
                    for what, *n in mamba_order():
                        if what == "split":
                            split(FIRST[l, "z"] + n[0])
                        elif what == "cs":
                            dve.wait_ge(cs_done, 1)
                            dve.tensor_copy(dt_u[:, 0, :], bank[6][:, 0:SSM_HEADS]).then_inc(cs_dec, 1)
                            dve.wait_ge(cs_dec, 1)
                            dve.tensor_tensor(decay[:, :], bank[6][:, 32:64], dt_u[:, 0, :], ALU.subtract).then_inc(cs_dec, 1)
                            dve.wait_ge(cs_exp, 2)
                            dve.tensor_tensor(decay[:, :], decay[:, :], dt[:, 0, :], ALU.mult).then_inc(dec_done, 1)
                        elif what == "x" and n[0] % 2 == 0:
                            dve.wait_ge(xt_done, n[0] + 1)
                            dve.tensor_copy(v(B_XTOK, 8, 512)[:, n[0], :], bank[4 + n[0] % 4][:, :]).then_inc(xtok_out_v, 1)
                        elif what == "first":
                            u, (g, c) = n[0], divmod(n[0], 2)
                            cbm = v(B_CBM + c * P, P)
                            dve.wait_ge(cb_done, u + 1)
                            if c == 0:
                                if g:
                                    dve.wait_ge(y_done, 2 * g - 1)
                                dve.tensor_copy(v(B_BTOK, P), bank[4][:, P:2 * P]).then_inc(btok_out, 1)
                            dve.tensor_tensor(cbm, bank[4][:, 0:P], tril[:, :], ALU.mult).then_inc(cbm_done, 1)
                            dve.wait_ge(cbm_done, u + 1)
                            dve.wait_ge(e_done, u + 1)
                            for k in range(HPG):
                                e = v(B_E + c * 512, HPG, P)[:, k, :]
                                ins = dve.scalar_tensor_tensor(out=e, in0=e, scalar=dt[:, c, HPG * g + k:HPG * g + k + 1], in1=cbm,
                                                               op0=ALU.mult, op1=ALU.mult)
                            ins.then_inc(m_done, 1)
                        elif what == "second":
                            u, (g, c) = n[0], divmod(n[0], 2)
                            y = y_all[:, c, g * GW:(g + 1) * GW]
                            dve.wait_ge(y_done, u + 1)
                            dve.wait_ge(xd_done, u + 1)
                            dve.tensor_tensor(y, bank[6][:, 0:GW], v(B_XD + c * 256, 256), ALU.add).then_inc(y_out, 1)
                            if c:
                                dve.tensor_tensor(v(B_TMP, HPG, HD), bank[6][:, GW:2 * GW].rearrange("p (h d) -> p h d", d=HD),
                                                  ecs[:, HPG * g:HPG * g + HPG].unsqueeze(2).to_broadcast([P, HPG, HD]), ALU.mult).then_inc(ycomb, 1)
                                dve.wait_ge(ycomb, g + 1)
                                dve.wait_ge(y_out, u + 1)
                                dve.tensor_tensor(y, y, v(B_TMP, 256), ALU.add).then_inc(y_whole, 1)
                        elif what == "turn":
                            g = n[0]
                            dve.wait_ge(xhi_done, T_FIRST[l, "mix"] + g + 1)
                            for k in range(2):
                                ins = dve.scalar_tensor_tensor(out=xt[:, 1, mix_slot(2 * g + k), :], in0=bank[7][:, k * SEQ:(k + 1) * SEQ],
                                                               scalar=gnw[:, 2 * g + k:2 * g + k + 1],
                                                               in1=xt[:, 0, mix_slot(2 * g + k), :].bitcast(F32), op0=ALU.mult, op1=ALU.subtract)
                            ins.then_inc(xlo_done, 1)
                    residual((l, "mlp"), FIRST[l, "out"] + 8, 2 * MLP_STEPS + 4)
                else:
                    attention(l)
                if l % 3 != 1:
                    split(FIRST[l, "mlp"] - 1 + LEAD)
                    scale((l, "mlp"), 1)
                    t_lo_norm((l, "mlp"), 1)
                mlp(l)
                with dve.Fori(0, MLP_STEPS - 2) as i:
                    mlp(l, i, 1)
                mlp(l, None, MLP_STEPS - 1)
                residual((l + 1, "norm") if l + 1 < DEPTH else "final", FIRST[l, "mlp"] + MLP_STEPS * MLP_PER, 2 * MLP_STEPS * (l + 1) + 4 * (l >= 1))

        @block.tensor
        def _(pe):
            def mm(dst, lhs, rhs, start, stop):
                return pe.matmul(dst, lhs, rhs, start=start, stop=stop)

            def transposed(name, j, src, b):
                for t in range(NT):
                    for k in range(2):
                        ins = pe.transpose(bank[b][:, k * SEQ + t * P:k * SEQ + (t + 1) * P],
                                           src[:, t, (2 * j + k) * P:(2 * j + k + 1) * P], ident[:, :])
                ins.then_inc(t_done, 1)

            def transposed_norm(name, t):
                pe.wait_ge(xs_done, NT * NORMS[name] + t + 1)
                for n in range(2):
                    for k in range(4):
                        ins = pe.transpose(bank[4 + 2 * t + n][:, k * P:(k + 1) * P], xs[:, t, (4 * n + k) * P:(4 * n + k + 1) * P], ident[:, :])
                    ins.then_inc(t_done, 1)

            def features(c, b, i=None, per=0, between=None):
                pe.wait_ge(lo_done, of(c + 1, i, per))
                hi = w_hi[:, c % RING, :].rearrange("p (k n) -> p k n", k=KT)
                lo = w_lo[:, c % RING, :].rearrange("p (k n) -> p k n", k=KT)
                for e in range(2):
                    if e and between:
                        between()
                    for k in range(KT):
                        for n, (s, w) in enumerate(((0, hi), (1, hi), (0, lo))):
                            ins = pe.matmul(bank[b][:, e * SEQ:(e + 1) * SEQ], w[:, k, e * P:(e + 1) * P], xt[:, s, k, :],
                                            start=k == 0 and n == 0, stop=k == KT - 1 and n == 2)
                ins.then_inc(chunk_done, 1)

            def first_tokens(name, c, b):
                pe.wait_ge(lo_done, c + 1)
                for t in range(NT):
                    for j in range(2):
                        if (t, j) == (0, 1):
                            pe.wait_ge(lo_done, c + 2)
                        hi = w_hi[:, (c + j) % RING, :].rearrange("p (k n) -> p k n", k=KT)
                        lo = w_lo[:, (c + j) % RING, :].rearrange("p (k n) -> p k n", k=KT)
                        for k in range(KT):
                            if (t, j, k) == (0, 1, 4):
                                transposed_norm(name, 1)
                            if j == 0 and k % 4 == 0:
                                pe.wait_ge(xlo_done, T_FIRST[name] + 2 * t + k // 4 + 1)
                            for n, (s, w) in enumerate(((0, hi), (1, hi), (0, lo))):
                                ins = pe.matmul(bank[b + j][:, t * 256:(t + 1) * 256], xt[:, s, k, t * P:(t + 1) * P], w[:, k, :],
                                                start=k == 0 and n == 0, stop=k == KT - 1 and n == 2)
                        if t:
                            ins.then_inc(chunk_done, 1)

            def turn_square(l, k):
                pe.wait_ge(sq_done, 16 * l + k + 1)
                for e in range(2):
                    for t in range(NT):
                        ins = pe.transpose(bank[4 + k][:, e * SEQ + t * P:e * SEQ + (t + 1) * P],
                                           v(M_SQ, 4, NT, 256)[:, k, t, e * P:(e + 1) * P], ident[:, :])
                ins.then_inc(sqt_done, 1)

            def part(c, k0, t, nb, ks, first, last):
                hi = w_hi[:, (c + nb) % RING, :].rearrange("p (k n) -> p k n", k=4)
                lo = w_lo[:, (c + nb) % RING, :].rearrange("p (k n) -> p k n", k=4)
                for k in ks:
                    for n, (s, w) in enumerate(((0, hi), (1, hi), (0, lo))):
                        ins = pe.matmul(bank[2 * nb + t][:, :], xt[:, s, k0 + k, t * P:(t + 1) * P], w[:, k, :],
                                        start=first and k == 0 and n == 0, stop=last and k == 3 and n == 2, skip_group_check=True)
                if ks[-1] == 3 and t:
                    ins.then_inc(chunk_done, 1)
                elif ks[-1] == 3 and nb:
                    ins.then_inc(tile_done, 1)

            def two_chunks(c, k0, i=None, per=0, first=False, last=False, turn=None):
                pe.wait_ge(lo_done, of(c + 2, i, per))
                for t in range(NT):
                    for nb in range(2):
                        if turn and t and nb:
                            part(c, k0, t, nb, range(0, 3), first, last)
                            transposed_norm(turn, 0)
                            part(c, k0, t, nb, range(3, 4), first, last)
                        else:
                            part(c, k0, t, nb, range(0, 4), first, last)

            def attention(l):
                ng = 1 if l % 3 == 0 else C_GROUPS
                u0, h0, w = UNIT0[l], HEAD0[l], 3 * P * ng
                slots = 4 if ng == 1 else 3
                sm = v(AT_SM, slots, w)
                c, a, name = FIRST[l, "qkv"], l // 3, (l, "norm")

                def q_of(n, g):
                    at = slice(64 * (n % 2), 64 * (n % 2) + 64)
                    if ng == 1:
                        return v(A_QT, 8, SEQ)[at, n // 2, :]
                    return v(C_QT + n // QUAD % 2 * 1536, C_GROUPS, 2, SEQ)[at, g, n % QUAD // 2, :]

                def k_of(n, g):
                    at = slice(64 * (n % 2), 64 * (n % 2) + 64)
                    if ng == 1:
                        return v(A_KT, 2, SEQ)[at, n // 8, :]
                    return v(C_KT + n // QUAD % 2 * 1536, C_GROUPS, 2, SEQ)[at, g, n % QUAD // 2, :]

                def v_of(n, g, t):
                    if ng == 1:
                        return v(A_V, NT, P)[:, t, n // 8 * HD:n // 8 * HD + HD]
                    k = n % QUAD * HD
                    return v(C_V + n // QUAD % 2 * 1536, NT, C_GROUPS, QW)[:, t, g, k:k + HD]

                def scores(u):
                    n, g = u // ng, u % ng
                    if n % QUAD == 0 and g == 0:
                        last = 1 + n // QUAD if ng == 1 else 9 * (n // QUAD) + 5
                        pe.wait_ge(qt_out, ROPE_NO[l, last] + 1)
                    if u >= 2:
                        pe.wait_ge(sm_done, 2 * (u0 + u - 1))
                    q, k = q_of(n, g), k_of(n, g)
                    mm(bank[4 + u % 2][:, 0:P], q[:, 0:P], k[:, 0:P], True, True)
                    mm(bank[4 + u % 2][:, P:3 * P], q[:, P:2 * P], k[:, 0:2 * P], True, True).then_inc(sc_done, 1)

                def turn(u):
                    n, g = u // ng, u % ng
                    if g == 0:
                        pe.wait_ge(pr_done, 2 * (h0 + n + 1))
                    if u:
                        pe.wait_ge(pt_out, u0 + u)
                    for m, at in enumerate((P * g, P * ng + 2 * P * g, P * ng + 2 * P * g + P)):
                        ins = pe.transpose(bank[6][:, m * P:(m + 1) * P], sm[:, n % slots, at:at + P], ident[:, :])
                    ins.then_inc(pt_done, 1)

                def values(u):
                    n, g = u // ng, u % ng
                    q = n // QUAD
                    b = bank[2 + q % 2]
                    if n % QUAD == 0 and g == 0:
                        if q >= 2:
                            pe.wait_ge(o_out, QUAD0[l] + q - 1)
                        if ng > 1:
                            pe.wait_ge(v_out, V_NO[l, 9 * q + 8] + 1)
                        for e in range(2):
                            pe.matmul(b[:, e * QW:(e + 1) * QW], zero16[:, :], tril[:, :].bitcast(BF16), start=e == 0, stop=False,
                                      skip_group_check=True)
                    pe.wait_ge(pt_out, u0 + u + 1)
                    pt = v(AT_PT + u % 3 * 384, 3, P)
                    at = n % QUAD * HD
                    for m, (o, t) in enumerate(((at, 0), (QW + at, 0), (QW + at, 1))):
                        ins = pe.matmul(b[:, o:o + HD], pt[:, m, :], v_of(n, g, t), start=False, stop=False, skip_group_check=True)
                    ins.then_inc(pv_done, 1)

                def bank_free(b):
                    if ng == 1:
                        pe.wait_ge(biased, NT * (A_BLOCKS * a + b + 1))
                    elif is_rotated(l, b):
                        pe.wait_ge(rope_mul, NT * (ROPE_NO[l, b] + 1))
                    else:
                        pe.wait_ge(v_out, V_NO[l, b] + 1)

                blocks = A_BLOCKS if ng == 1 else 9 * QUADS
                bank7 = [None]
                for step in order(l):
                    what, q, m = step[0], step[1], step[-1]
                    if what == "piece":
                        t, k0 = m // 2, 4 * (m % 2)
                        if (l, q, m) == (0, 0, 0):
                            pe.wait_ge(first_lo, 1)
                        elif m == 0 or (l, q, m) == (0, 0, 1):
                            pe.wait_ge(lo_done, c + q + 1)
                        if m == 0:
                            if bank_before(q) is not None:
                                bank_free(bank_before(q))
                        if q == 0:
                            pe.wait_ge(xlo_done, T_FIRST[name] + m + 1)
                        hi = w_hi[:, (c + q) % RING, :].rearrange("p (k n) -> p k n", k=KT)
                        lo = w_lo[:, (c + q) % RING, :].rearrange("p (k n) -> p k n", k=KT)
                        for k in range(k0, k0 + 4):
                            for n, (s, w_) in enumerate(((0, hi), (1, hi), (0, lo))):
                                ins = pe.matmul(bank[block_bank(q)][:, t * QW:(t + 1) * QW], xt[:, s, k, t * P:(t + 1) * P], w_[:, k, :],
                                                start=k == 0 and n == 0, stop=k == KT - 1 and n == 2)
                        if m == 3:
                            ins.then_inc(chunk_done, 1)
                    elif what == "turn":
                        transposed_norm(name, 1)
                        if l == 0:
                            conv_columns()
                    elif what == "turn_next":
                        pe.wait_ge(sm_done, 2 * (u0 + A_HEADS * ng))
                        transposed_norm((l, "mlp"), 0)
                    elif what == "opiece":
                        t, nb, n = m // 2, m % 2, 4 * min(q, 2) + m
                        cc = FIRST[l, "o"] + q
                        if m == 0:
                            pe.wait_ge(lo_done, cc + 1)
                            pe.wait_ge(xlo_done, T_FIRST[l, "mix"] + q + 1)
                        if n < 2:
                            bank_free(blocks - 2 + n)
                        elif q < 3:
                            pe.wait_ge(h_done, H_END[l, "mix"] - O_ADDS + n - 1)
                        hi = w_hi[:, cc % RING, :].rearrange("p (k n) -> p k n", k=2)
                        lo = w_lo[:, cc % RING, :].rearrange("p (k n) -> p k n", k=2)
                        for k in range(2):
                            for e, (s, w_) in enumerate(((0, hi), (1, hi), (0, lo))):
                                ins = pe.matmul(bank[obank(l, n)][:, :], xt[:, s, KT + 2 * q + k, t * P:(t + 1) * P],
                                                w_[:, k, nb * 512:(nb + 1) * 512], start=q < 3 and k == 0 and e == 0, stop=q != 2 and k == 1 and e == 2)
                        if m == 3:
                            ins.then_inc(chunk_done, 1)
                        elif q != 2:
                            ins.then_inc(wo_done, 1)
                    elif what == "tq":
                        n = ROPE_NO[l, q]
                        if bank7[0]:
                            pe.wait_ge(*bank7[0])
                        pe.wait_ge(roped, NT * (n + 1))
                        src = v(AT_ROT + (n % 2) * 512, NT, 256)
                        for k in range(2):
                            for t in range(NT):
                                ins = pe.transpose(bank[7][:, k * SEQ + t * P:k * SEQ + (t + 1) * P], src[:, t, k * P:(k + 1) * P], ident[:, :])
                        ins.then_inc(qt_done, 1)
                        bank7[0] = (qt_out, n + 1)
                    elif what == "mix":
                        if bank7[0]:
                            pe.wait_ge(*bank7[0])
                        pe.wait_ge(o_out, QUAD0[l] + q + 1)
                        transposed((l, "mix"), q, xs, 7)
                        bank7[0] = (xlo_done, T_FIRST[l, "mix"] + q + 1)
                    elif what == "event":
                        s_, t_, v_ = event_units(l, q, m)
                        if t_ is not None:
                            turn(t_)
                        if s_ is not None:
                            scores(s_)
                        if v_ is not None:
                            values(v_)

            def conv_columns():
                pe.wait_ge(in_small, 16 * SMALL_LOADS)
                pe.transpose(bank[3][:, 0:P], convw_rows, ident[:, :])
                pe.transpose(bank[3][:, P:P + CT_ALL], convb_rows, ident[0:CT_ALL, 0:CT_ALL])
                pe.transpose(bank[3][:, P + CT_ALL:P + CT_ALL + CT_X], gnw_rows, ident[0:CT_X, 0:CT_X]).then_inc(cols_done, 1)

            pe.wait_ge(pool_const, 4)
            pe.wait_ge(vec_const, 1)
            pe.transpose(bank[3][:, 2 * P:2 * P + NT], pos_rows_f, ident[0:NT, 0:NT]).then_inc(cols_done, 1)
            transposed_norm((0, "norm"), 0)
            for l in range(DEPTH):
                if l % 3 != 1:
                    attention(l)
                else:
                    c = FIRST[l, "xbc"]

                    def z_piece(nb, k, t, half):
                        c = z_chunk(l, nb, k)
                        hi = w_hi[:, c % RING, :].rearrange("p (k n) -> p k n", k=4)
                        lo = w_lo[:, c % RING, :].rearrange("p (k n) -> p k n", k=4)
                        for kk in (2 * half, 2 * half + 1):
                            for e, (s, w) in enumerate(((0, hi), (1, hi), (0, lo))):
                                ins = pe.matmul(bank[2 * (nb % 2) + t][:, :], xt[:, s, 4 * k + kk, t * P:(t + 1) * P], w[:, kk, :],
                                                start=(k, kk, e) == (0, 0, 0), stop=(k, kk, e) == (1, 3, 2))
                        if (t, half) == (1, 1):
                            ins.then_inc(chunk_done, 1)

                    for t in range(NT):
                        for k in range(2):
                            if t == 0:
                                pe.wait_ge(lo_done, z_chunk(l, 0, k) + 1)
                            pe.wait_ge(xlo_done, T_FIRST[l, "norm"] + 2 * t + k + 1)
                            z_piece(0, k, t, 0)
                            if (t, k) == (0, 1):
                                transposed_norm((l, "norm"), 1)
                            z_piece(0, k, t, 1)
                    d = FIRST[l, "dt"]
                    pe.wait_ge(lo_done, d + 1)
                    pe.wait_ge(h_done, H_END[l - 1, "mlp"])
                    hi = w_hi[:, d % RING, 0:KT * SSM_HEADS].rearrange("p (k n) -> p k n", k=KT)
                    lo = w_lo[:, d % RING, 0:KT * SSM_HEADS].rearrange("p (k n) -> p k n", k=KT)
                    for t in range(NT):
                        for k in range(KT):
                            for e, (s, w) in enumerate(((0, hi), (1, hi), (0, lo))):
                                ins = pe.matmul(bank[2 + t][:, 0:SSM_HEADS], xt[:, s, k, t * P:(t + 1) * P], w[:, k, :],
                                                start=k == 0 and e == 0, stop=k == KT - 1 and e == 2)
                    ins.then_inc(chunk_done, 1)

                    for j in range(4):
                        features(c + j, 4 + j)
                    with pe.Fori(0, 3) as i:
                        for j in range(4):
                            pe.wait_ge(pad_done, of(4 + j + 1, i, 4))
                            features(c + 4 + j, 4 + j, i, 4)
                    xc, xtok = v(B_XC, CT_ALL, SEQ), v(B_XTOK, NT, INNER)
                    bt, ct = v(B_BT, GROUPS, SEQ), v(B_CT, GROUPS, SEQ)
                    for what, *n in mamba_order():
                        if what == "cs":
                            pe.wait_ge(dt_done, 2)
                            pe.wait_ge(xtok_out_v, 4)
                            pe.wait_ge(xtok_out_a, 4)
                            mm(bank[6][:, 0:32], tril[:, :], da[:, 0, :], True, True)
                            mm(bank[6][:, 32:64], ones[:, :], da[:, 0, :], True, True)
                            mm(bank[7][:, 0:32], tril[:, :], da[:, 1, :], True, True).then_inc(cs_done, 1)
                        elif what == "x":
                            t, q = n[0] // 4, n[0] % 4
                            if n[0] == 0:
                                pe.wait_ge(conv_out, 9)
                            if n[0] < 4:
                                pe.wait_ge(pad_done, 17 + n[0])
                            else:
                                pe.wait_ge(xtok_out_a if n[0] % 2 else xtok_out_v, n[0] // 2 - 1)
                            for k in range(4):
                                ins = pe.transpose(bank[4 + n[0] % 4][:, k * P:(k + 1) * P], xc[:, 4 * q + k, t * P:(t + 1) * P], ident[:, :])
                            ins.then_inc(xt_done, 1)
                        elif what == "z":
                            nb, k, t, half = n
                            if (t, half) == (0, 0):
                                pe.wait_ge(lo_done, z_chunk(l, nb, k) + 1)
                            if (k, t, half) == (0, 0, 0):
                                if nb == 1:
                                    pe.wait_ge(dt_pre, 2)
                                else:
                                    pe.wait_ge(z_out, 2 * (nb - 1))
                            z_piece(nb, k, t, half)
                        elif what == "first":
                            u, (g, c) = n[0], divmod(n[0], 2)
                            tok = slice(c * P, (c + 1) * P)
                            if u == 0:
                                pe.wait_ge(conv_out, 17)
                            else:
                                pe.wait_ge(cbm_done, u)
                            if c == 0:
                                pe.transpose(bank[4][:, P:2 * P], bt[:, g, 0:P], ident[:, :])
                            mm(bank[4][:, 0:P], bt[:, g, tok], ct[:, g, tok], True, True).then_inc(cb_done, 1)
                            pe.wait_ge(rl_done, u + 1)
                            if u:
                                pe.wait_ge(e_done, u)
                            mm(bank[5][:, :], strict[:, :], v(B_RL, 512), True, True).then_inc(seg_done, 1)
                        elif what == "second":
                            u, (g, c) = n[0], divmod(n[0], 2)
                            if u:
                                pe.wait_ge(y_out, u)
                            else:
                                pe.wait_ge(cs_dec, 2)
                            pe.wait_ge(m_done, u + 1)
                            if c == 0:
                                if g:
                                    pe.wait_ge(ycomb, g)
                                pe.wait_ge(btok_out, g + 1)
                                pe.wait_ge(xdec_done, g + 1)
                            else:
                                pe.wait_ge(st_out, g + 1)
                            for k in range(HPG):
                                mm(bank[6][:, k * HD:(k + 1) * HD], v(B_E + c * 512, HPG, P)[:, k, :],
                                   xtok[:, c, g * GW + k * HD:g * GW + (k + 1) * HD], True, True)
                            if c == 0:
                                ins = mm(bank[6][:, GW:2 * GW], v(B_BTOK, P), v(B_XDEC + (g % 2) * 256, 256), True, True)
                            else:
                                ins = mm(bank[6][:, GW:2 * GW], ct[:, g, P:2 * P], v(B_ST + (g % 2) * 256, 256), True, True)
                            ins.then_inc(y_done, 1)
                        elif what == "turn":
                            pe.wait_ge(gn_done, n[0] + 1)
                            if n[0]:
                                pe.wait_ge(xlo_done, T_FIRST[l, "mix"] + n[0])
                            transposed((l, "mix"), n[0], v(B_G, NT, INNER), 7)
                        elif what == "out":
                            k, t, nb, half = n
                            c = FIRST[l, "out"] + 2 * k
                            if (t, half) == (0, 0):
                                pe.wait_ge(lo_done, c + nb + 1)
                                if (k, nb) == (0, 1):
                                    pe.wait_ge(z_out, 8)
                            if (t, nb) == (0, 0):
                                pe.wait_ge(xlo_done, T_FIRST[l, "mix"] + 2 * k + half + 1)
                            ks = range(2 * half, 2 * half + 2)
                            if (k, t, nb, half) == (3, 1, 1, 1):
                                part(c, mix_slot(4 * k), t, nb, ks[:1], k == 0, k == 3)
                                transposed_norm((l, "mlp"), 0)
                                ks = ks[1:]
                            part(c, mix_slot(4 * k), t, nb, ks, k == 0, k == 3)
                after = ((l + 1, "norm") if l + 1 < DEPTH else None)

                def mlp(i, step0):
                    c, u = FIRST[l, "mlp"] + step0 * MLP_PER, 16 * l + 4 * step0
                    if step0 == 0:
                        first_tokens((l, "mlp"), c, 4)
                        pe.wait_ge(h_done, H_END[l, "mix"])
                    for j in range(2 if step0 == 0 else 0, 4):
                        features(c + j, 4 + j, i, MLP_PER, between=(lambda k=j - 2: turn_square(l, k)) if step0 == 0 else None)
                    for f in range(2):
                        pe.wait_ge(ulo_done, of(u + 2 * f + 2, i, 4))
                        two_chunks(c + 4 + 2 * f, KT + 4 * f, i, MLP_PER,
                                   first=(step0, f) == (0, 0), last=(step0, f) == (MLP_STEPS - 1, 1),
                                   turn=after if step0 == MLP_STEPS - 1 and f == 1 else None)

                mlp(None, 0)
                with pe.Fori(0, MLP_STEPS - 2) as i:
                    mlp(i, 1)
                mlp(None, MLP_STEPS - 1)


_INS = ["x", "positions", "norm_mix_w", "norm_mlp_w", "a_w_qkv", "a_b_qkv", "a_sinks", "a_w_o", "a_b_o",
        "b_in_w", "b_conv_w", "b_conv_b", "b_dt_bias", "b_a_log", "b_d", "b_norm_w", "b_out_w",
        "c_w_qkv", "c_w_o", "mlp_w_up", "mlp_w_down", "final_norm_w"]


def kernel(**inputs):
    import numpy as _np
    import concourse.bacc as _bacc
    from concourse import mybir as _mybir
    from concourse.bass_utils import run_bass_kernel_spmd as _run

    nc = _bacc.Bacc("TRN2", target_bir_lowering=False, num_devices=1)
    arrays, args = {}, []

    def give(name, a):
        arrays[f"in_{name}"] = a
        args.append(nc.dram_tensor(f"in_{name}", a.shape, _mybir.dt.from_np(a.dtype), kind="ExternalInput").ap())

    for name in _INS:
        give(name, _np.ascontiguousarray(inputs[name]))
    give("rope_freq", (10000.0 ** (-_np.arange(HALF, dtype=_np.float32) / _np.float32(HALF))).astype(_np.float32))
    args.append(nc.dram_tensor("out", (1, SEQ, D), F32, kind="ExternalOutput").ap())
    trunk(nc, *args)
    r = _run(nc, [arrays], core_ids=[0])
    return r.results[0]["out"]
```
